# Optimizing a Trainium2 kernel written in Bass

```python
import jax, jax.numpy as jnp
from jax import lax
import numpy as np
import math

D_MODEL = 1024
BATCH = 1
SEQ = 1024
DEPTH = 1

N_MIXERS = 3
RMS_EPS = 1e-6
BLOCK = 128
NEG = -1e30

SWA_HEAD_DIM = 64
SWA_HEADS = D_MODEL // SWA_HEAD_DIM
SWA_KV_HEADS = SWA_HEADS // 8
SWA_GROUP = SWA_HEADS // SWA_KV_HEADS
WINDOW = 128

SB_HEAD_DIM = 64
SB_HEADS = D_MODEL // SB_HEAD_DIM

RET_QK_DIM = 256
RET_HEADS = D_MODEL // RET_QK_DIM
RET_V_DIM = 2 * RET_QK_DIM

D_FF = 4 * D_MODEL

N_A = len(range(0, DEPTH, N_MIXERS))
N_B = len(range(1, DEPTH, N_MIXERS))
N_C = len(range(2, DEPTH, N_MIXERS))


def rms_norm(x, g):
    xf = x.astype(jnp.float32)
    y = xf * lax.rsqrt(jnp.mean(xf * xf, axis=-1, keepdims=True) + RMS_EPS)
    return (y * g.astype(jnp.float32)).astype(x.dtype)

def alibi_slopes(n_heads):
    return jnp.exp2(-8.0 * jnp.arange(1, n_heads + 1, dtype=jnp.float32) / n_heads)

def swa_mixer(h, w_qkv, sinks, w_o):
    B_, T, _ = h.shape
    nb = T // BLOCK
    HD, KV, G = SWA_HEAD_DIM, SWA_KV_HEADS, SWA_GROUP
    qkv = h @ w_qkv
    q, k, v = jnp.split(qkv, [SWA_HEADS * HD, (SWA_HEADS + KV) * HD], axis=-1)
    q = q.reshape(B_, nb, BLOCK, KV, G, HD)
    k = k.reshape(B_, nb, BLOCK, KV, HD)
    v = v.reshape(B_, nb, BLOCK, KV, HD)

    def with_prev(a):
        prev = jnp.pad(a, ((0, 0), (1, 0), (0, 0), (0, 0), (0, 0)))[:, :-1]
        return jnp.concatenate([prev, a], axis=2)

    kb, vb = with_prev(k), with_prev(v)
    s = jnp.einsum('bnqkgd,bnskd->bnkgqs', q, kb).astype(jnp.float32) * (HD ** -0.5)

    blk = jnp.arange(nb)[:, None, None]
    qi = jnp.arange(BLOCK)[None, :, None]
    kj = jnp.arange(2 * BLOCK)[None, None, :]
    dist = BLOCK + qi - kj
    kpos = (blk - 1) * BLOCK + kj
    mask = (dist >= 0) & (dist < WINDOW) & (kpos >= 0)
    slopes = alibi_slopes(SWA_HEADS).reshape(1, 1, KV, G, 1, 1)
    bias = -slopes * dist.astype(jnp.float32)[None, :, None, None]
    logits = jnp.where(mask[None, :, None, None], s + bias, NEG)

    sink = sinks.astype(jnp.float32).reshape(1, 1, KV, G, 1, 1)
    m = jnp.maximum(jnp.max(logits, axis=-1, keepdims=True), sink)
    p = jnp.exp(logits - m)
    probs = p / (jnp.sum(p, axis=-1, keepdims=True) + jnp.exp(sink - m))
    o = jnp.einsum('bnkgqs,bnskd->bnqkgd', probs.astype(vb.dtype), vb)
    return o.reshape(B_, T, SWA_HEADS * HD) @ w_o

def stick_breaking_mixer(h, w_qkv, w_o):
    B_, T, _ = h.shape
    HD, H = SB_HEAD_DIM, SB_HEADS
    qkv = (h @ w_qkv).reshape(B_, T, 3, H, HD)
    q = jnp.transpose(qkv[:, :, 0], (0, 2, 1, 3))
    k = jnp.transpose(qkv[:, :, 1], (0, 2, 1, 3))
    v = jnp.transpose(qkv[:, :, 2], (0, 2, 1, 3))
    scale = HD ** -0.5
    outs = []
    for n in range(T // BLOCK):
        q0, end = n * BLOCK, (n + 1) * BLOCK
        z = jnp.einsum('bhqd,bhsd->bhqs', q[:, :, q0:end], k[:, :, :end]).astype(jnp.float32) * scale
        t_pos = q0 + jnp.arange(BLOCK)[:, None]
        s_pos = jnp.arange(end)[None, :]
        causal = (s_pos < t_pos)[None, None]
        log_beta = jax.nn.log_sigmoid(z)
        log_1m_beta = jnp.where(causal, jax.nn.log_sigmoid(-z), 0.0)
        rest = lax.cumsum(log_1m_beta, axis=3, reverse=True) - log_1m_beta
        a = jnp.where(causal, jnp.exp(log_beta + rest), 0.0)
        outs.append(jnp.einsum('bhqs,bhsd->bhqd', a.astype(v.dtype), v[:, :, :end]))
    o = jnp.concatenate(outs, axis=2)
    return jnp.transpose(o, (0, 2, 1, 3)).reshape(B_, T, H * HD) @ w_o

def retention_mixer(h, w_in, w_o):
    B_, T, _ = h.shape
    nc, C, H, dk, dv = T // BLOCK, BLOCK, RET_HEADS, RET_QK_DIM, RET_V_DIM
    proj = h @ w_in
    q, k, v, g = jnp.split(proj, [H * dk, 2 * H * dk, 2 * H * dk + H * dv], axis=-1)
    q = q.astype(jnp.float32).reshape(B_, nc, C, H, dk)
    k = k.astype(jnp.float32).reshape(B_, nc, C, H, dk) * (dk ** -0.5)
    v = v.astype(jnp.float32).reshape(B_, nc, C, H, dv)

    log_gamma = jnp.log1p(-jnp.exp2(-5.0 - jnp.arange(H, dtype=jnp.float32)))
    idx = jnp.arange(C)
    diff = idx[:, None] - idx[None, :]
    decay_mat = jnp.where(diff >= 0,
                          jnp.exp(log_gamma[:, None, None] * jnp.maximum(diff, 0).astype(jnp.float32)),
                          0.0)
    scores = jnp.einsum('bnihd,bnjhd->bnhij', q, k) * decay_mat
    o_inner = jnp.einsum('bnhij,bnjhe->bnihe', scores, v)
    q_decay = jnp.exp(log_gamma[:, None] * (idx + 1).astype(jnp.float32))
    k_decay = jnp.exp(log_gamma[:, None] * (C - 1 - idx).astype(jnp.float32))
    chunk_decay = jnp.exp(log_gamma * C)[None, :, None, None]
    kv_chunk = jnp.einsum('bnjhd,hj,bnjhe->bnhde', k, k_decay, v)

    def step(state, kv_n):
        return state * chunk_decay + kv_n, state

    init = jnp.zeros((B_, H, dk, dv), jnp.float32)
    _, prev_states = lax.scan(step, init, jnp.moveaxis(kv_chunk, 1, 0))
    prev_states = jnp.moveaxis(prev_states, 0, 1)
    o_cross = jnp.einsum('bnihd,hi,bnhde->bnihe', q, q_decay, prev_states)
    o = o_inner + o_cross
    o = o * lax.rsqrt(jnp.mean(o * o, axis=-1, keepdims=True) + RMS_EPS)
    o = o.reshape(B_, T, H * dv)
    y = jax.nn.silu(g.astype(jnp.float32)) * o
    return y.astype(h.dtype) @ w_o

def squared_relu_mlp(h, w_up, w_down):
    a = jax.nn.relu(h @ w_up)
    return (a * a) @ w_down

def first_inputs(seed: int = 0) -> dict:
    key = jax.random.key(seed)
    ks = jax.random.split(key, 16)

    def dense(k, shape):
        return jax.random.normal(k, shape, jnp.float32) * (shape[-2] ** -0.5)

    def gain(k, shape):
        return 1.0 + 0.02 * jax.random.normal(k, shape, jnp.float32)

    swa_qkv_dim = (SWA_HEADS + 2 * SWA_KV_HEADS) * SWA_HEAD_DIM
    ret_in_dim = 2 * RET_HEADS * RET_QK_DIM + 2 * RET_HEADS * RET_V_DIM
    return {
        "x": jax.random.normal(ks[0], (BATCH, SEQ, D_MODEL), jnp.float32),
        "attn_norm": gain(ks[1], (DEPTH, D_MODEL)),
        "mlp_norm": gain(ks[2], (DEPTH, D_MODEL)),
        "final_norm": gain(ks[3], (D_MODEL,)),
        "swa_w_qkv": dense(ks[4], (N_A, D_MODEL, swa_qkv_dim)),
        "swa_sinks": 0.5 * jax.random.normal(ks[5], (N_A, SWA_HEADS), jnp.float32),
        "swa_w_o": dense(ks[6], (N_A, SWA_HEADS * SWA_HEAD_DIM, D_MODEL)),
        "sb_w_qkv": dense(ks[7], (N_B, D_MODEL, 3 * SB_HEADS * SB_HEAD_DIM)),
        "sb_w_o": dense(ks[8], (N_B, SB_HEADS * SB_HEAD_DIM, D_MODEL)),
        "ret_w_in": dense(ks[9], (N_C, D_MODEL, ret_in_dim)),
        "ret_w_o": dense(ks[10], (N_C, RET_HEADS * RET_V_DIM, D_MODEL)),
        "mlp_w_up": dense(ks[11], (DEPTH, D_MODEL, D_FF)),
        "mlp_w_down": dense(ks[12], (DEPTH, D_FF, D_MODEL)),
    }

def first_block(x, attn_norm, mlp_norm, final_norm, swa_w_qkv, swa_sinks, swa_w_o,
              sb_w_qkv, sb_w_o, ret_w_in, ret_w_o, mlp_w_up, mlp_w_down):
    h = x
    for i in range(DEPTH):
        kind, j = i % N_MIXERS, i // N_MIXERS
        u = rms_norm(h, attn_norm[i])
        if kind == 0:
            mix = swa_mixer(u, swa_w_qkv[j], swa_sinks[j], swa_w_o[j])
        elif kind == 1:
            mix = stick_breaking_mixer(u, sb_w_qkv[j], sb_w_o[j])
        else:
            mix = retention_mixer(u, ret_w_in[j], ret_w_o[j])
        h = h + mix
        h = h + squared_relu_mlp(rms_norm(h, mlp_norm[i]), mlp_w_up[i], mlp_w_down[i])
    return rms_norm(h, final_norm)


GRID_W = 64
CTX_LEN = 256
MLA_HEADS = 8
QK_NOPE = 64
QK_ROPE = 32
QK_DIM = QK_NOPE + QK_ROPE
V_DIM = 64
Q_LORA = 384
KV_LORA = 256
ROPE_THETA = 10000.0
Q_BLOCK = 128
F_GROUPS = 4
F_GROUP_DIM = 128
D_F = F_GROUPS * F_GROUP_DIM
OFF_Q = 0
OFF_KV = OFF_Q + Q_LORA
OFF_KPE = OFF_KV + KV_LORA
OFF_F = OFF_KPE + QK_ROPE
OFF_GA = OFF_F + D_F
OFF_GB = OFF_GA + D_MODEL
N_IN = OFF_GB + D_MODEL
N_EXPERTS = 16
D_EXPERT = 512
CAPACITY_FACTOR = 2
EPS = 1e-6


def _rms(x, g):
    xf = x.astype(jnp.float32)
    y = xf * lax.rsqrt(jnp.mean(xf * xf, axis=-1, keepdims=True) + EPS)
    return (y * g.astype(jnp.float32)).astype(x.dtype)

def _modulate(h, shift, scale):
    return h * (1.0 + scale) + shift

def _axial_tables(pos_row, pos_col, dtype):
    half = QK_ROPE // 2
    n_freq = half // 2
    inv_freq = 1.0 / (ROPE_THETA ** (jnp.arange(n_freq, dtype=jnp.float32) / n_freq))

    def tab(pos):
        ang = pos.astype(jnp.float32)[:, None] * inv_freq[None, :]
        ang = jnp.concatenate([ang, ang], axis=-1)[None, :, None, :]
        return jnp.cos(ang).astype(dtype), jnp.sin(ang).astype(dtype)

    cr, sr = tab(pos_row)
    cc, scol = tab(pos_col)
    return cr, sr, cc, scol

def _rope_axis(x, cos, sin):
    x1, x2 = jnp.split(x, 2, axis=-1)
    return x * cos + jnp.concatenate([-x2, x1], axis=-1) * sin

def _rope_2d(x, tabs):
    cr, sr, cc, scol = tabs
    xr, xc = jnp.split(x, 2, axis=-1)
    return jnp.concatenate([_rope_axis(xr, cr, sr), _rope_axis(xc, cc, scol)], axis=-1)

def _mla_qkv(p, q_a_g, kv_a_g, w_q_up, w_kv_up, q_g, k_g, tabs):
    B, T, _ = p.shape
    cq = _rms(p[..., OFF_Q:OFF_KV], q_a_g)
    ckv = _rms(p[..., OFF_KV:OFF_KPE], kv_a_g)
    k_pe = p[..., OFF_KPE:OFF_F]
    q = (cq @ w_q_up).reshape(B, T, MLA_HEADS, QK_DIM)
    kv = (ckv @ w_kv_up).reshape(B, T, MLA_HEADS, QK_NOPE + V_DIM)
    k_nope, v = kv[..., :QK_NOPE], kv[..., QK_NOPE:]
    k = jnp.concatenate([k_nope, jnp.broadcast_to(k_pe[:, :, None, :], (B, T, MLA_HEADS, QK_ROPE))], axis=-1)
    q = _rms(q, q_g)
    k = _rms(k, k_g)
    if tabs is not None:
        q = jnp.concatenate([q[..., :QK_NOPE], _rope_2d(q[..., QK_NOPE:], tabs)], axis=-1)
        k = jnp.concatenate([k[..., :QK_NOPE], _rope_2d(k[..., QK_NOPE:], tabs)], axis=-1)
    return q, k, v

def _attend_dense(q, k, v):
    s = jnp.einsum('bqhd,bkhd->bhqk', q, k, preferred_element_type=jnp.float32) * (QK_DIM ** -0.5)
    pr = jax.nn.softmax(s, axis=-1).astype(v.dtype)
    return jnp.einsum('bhqk,bkhd->bqhd', pr, v)

def _attend_latent(q, k_lat, v_lat, k_ctx, v_ctx):
    B, T, H, _ = q.shape
    k_all = jnp.concatenate([k_lat, k_ctx], axis=1)
    v_all = jnp.concatenate([v_lat, v_ctx], axis=1)
    nb = T // Q_BLOCK
    qb = jnp.moveaxis(q.reshape(B, nb, Q_BLOCK, H, QK_DIM), 1, 0)
    o = lax.map(lambda qi: _attend_dense(qi, k_all, v_all), qb)
    return jnp.moveaxis(o, 0, 1).reshape(B, T, H * V_DIM)

def _fourier(f):
    B, T, _ = f.shape
    fg = f.reshape(B, T, F_GROUPS, F_GROUP_DIM).astype(jnp.float32)
    y = jnp.fft.fft2(fg, axes=(1, 3), norm="ortho").real
    return y.reshape(B, T, D_F).astype(f.dtype)

def _expert_choice(h, w_r, w_g, w_u, w_d):
    B, T, D = h.shape
    cap = (CAPACITY_FACTOR * T) // N_EXPERTS
    logits = jnp.einsum('btd,de->bte', h, w_r, preferred_element_type=jnp.float32)
    aff = jax.nn.softmax(logits, axis=-1)
    gate, idx = lax.top_k(jnp.swapaxes(aff, 1, 2), cap)
    xe = jax.vmap(lambda hb, ib: hb[ib])(h, idx)
    a = jnp.einsum('becd,edf->becf', xe, w_g)
    u = jnp.einsum('becd,edf->becf', xe, w_u)
    ye = jnp.einsum('becf,efd->becd', jax.nn.silu(a) * u, w_d) * gate[..., None].astype(h.dtype)
    return jax.vmap(lambda yb, ib: jnp.zeros((T, D), yb.dtype).at[ib.reshape(-1)].add(yb.reshape(-1, D)))(ye, idx)

def _merge(p, attn_o, four_o, w_o_attn, w_fourier, w_out):
    ga = jax.nn.sigmoid(p[..., OFF_GA:OFF_GB])
    gb = jax.nn.sigmoid(p[..., OFF_GB:N_IN])
    return (ga * (attn_o @ w_o_attn) + gb * (four_o @ w_fourier)) @ w_out

def second_inputs(seed: int = 0) -> dict:
    key = jax.random.key(seed)
    ks = jax.random.split(key, 24)
    L, D = DEPTH, D_MODEL

    def nrm(k, shape, fan_in, mult=1.0):
        return jax.random.normal(k, shape, jnp.float32) * (mult * fan_in ** -0.5)

    def gain(k, shape):
        return 1.0 + 0.02 * jax.random.normal(k, shape, jnp.float32)

    return {
        "x": jax.random.normal(ks[0], (BATCH, SEQ, D), jnp.float32),
        "c": jax.random.normal(ks[1], (BATCH, D), jnp.float32),
        "ctx": jax.random.normal(ks[2], (BATCH, CTX_LEN, D), jnp.float32),
        "c_ctx": 0.5 * jax.random.normal(ks[3], (D,), jnp.float32),
        "w_mod": nrm(ks[4], (L, D, 6 * D), D, 0.5),
        "b_mod": 0.02 * jax.random.normal(ks[5], (L, 6 * D), jnp.float32),
        "norm1_g": gain(ks[6], (L, D)),
        "w_in": nrm(ks[7], (L, D, N_IN), D),
        "q_a_norm_g": gain(ks[8], (L, Q_LORA)),
        "kv_a_norm_g": gain(ks[9], (L, KV_LORA)),
        "w_q_up": nrm(ks[10], (L, Q_LORA, MLA_HEADS * QK_DIM), Q_LORA),
        "w_kv_up": nrm(ks[11], (L, KV_LORA, MLA_HEADS * (QK_NOPE + V_DIM)), KV_LORA),
        "q_norm_g": gain(ks[12], (L, QK_DIM)),
        "k_norm_g": gain(ks[13], (L, QK_DIM)),
        "w_o_attn": nrm(ks[14], (L, MLA_HEADS * V_DIM, D), MLA_HEADS * V_DIM),
        "w_fourier": nrm(ks[15], (L, D_F, D), D_F),
        "w_out": nrm(ks[16], (L, D, D), D),
        "norm2_g": gain(ks[17], (L, D)),
        "w_router": nrm(ks[18], (L, D, N_EXPERTS), D),
        "w_e_gate": nrm(ks[19], (L, N_EXPERTS, D, D_EXPERT), D),
        "w_e_up": nrm(ks[20], (L, N_EXPERTS, D, D_EXPERT), D),
        "w_e_down": nrm(ks[21], (L, N_EXPERTS, D_EXPERT, D), D_EXPERT),
    }

def second_block(x, c, ctx, c_ctx, w_mod, b_mod, norm1_g, w_in, q_a_norm_g, kv_a_norm_g,
              w_q_up, w_kv_up, q_norm_g, k_norm_g, w_o_attn, w_fourier, w_out, norm2_g,
              w_router, w_e_gate, w_e_up, w_e_down):
    T = x.shape[1]
    rows = T // GRID_W
    pos_row = jnp.repeat(jnp.arange(rows, dtype=jnp.int32), GRID_W)
    pos_col = jnp.tile(jnp.arange(GRID_W, dtype=jnp.int32), rows)
    tabs = _axial_tables(pos_row, pos_col, x.dtype)
    s_lat = jax.nn.silu(c)
    s_ctx = jax.nn.silu(c_ctx)

    for l in range(DEPTH):
        last = l == DEPTH - 1
        mod_l = (s_lat @ w_mod[l] + b_mod[l])[:, None, :]
        mod_c = s_ctx @ w_mod[l] + b_mod[l]
        sh1, sc1, g1, sh2, sc2, g2 = jnp.split(mod_l, 6, axis=-1)
        csh1, csc1, cg1, csh2, csc2, cg2 = jnp.split(mod_c, 6, axis=-1)

        h = _modulate(_rms(x, norm1_g[l]), sh1, sc1)
        hc = _modulate(_rms(ctx, norm1_g[l]), csh1, csc1)
        p = h @ w_in[l]
        pc = hc @ w_in[l]
        mla_w = (q_a_norm_g[l], kv_a_norm_g[l], w_q_up[l], w_kv_up[l], q_norm_g[l], k_norm_g[l])
        q, k, v = _mla_qkv(p, *mla_w, tabs)
        qc, kc, vc = _mla_qkv(pc, *mla_w, None)
        attn_lat = _attend_latent(q, k, v, kc, vc)
        four_lat = _fourier(p[..., OFF_F:OFF_GA])
        x = x + g1 * _merge(p, attn_lat, four_lat, w_o_attn[l], w_fourier[l], w_out[l])

        if not last:
            B = ctx.shape[0]
            attn_ctx = _attend_dense(qc, kc, vc).reshape(B, CTX_LEN, MLA_HEADS * V_DIM)
            four_ctx = _fourier(pc[..., OFF_F:OFF_GA])
            ctx = ctx + cg1 * _merge(pc, attn_ctx, four_ctx, w_o_attn[l], w_fourier[l], w_out[l])

        moe_w = (w_router[l], w_e_gate[l], w_e_up[l], w_e_down[l])
        h2 = _modulate(_rms(x, norm2_g[l]), sh2, sc2)
        x = x + g2 * _expert_choice(h2, *moe_w)
        if not last:
            hc2 = _modulate(_rms(ctx, norm2_g[l]), csh2, csc2)
            ctx = ctx + cg2 * _expert_choice(hc2, *moe_w)
    return x


def setup_inputs(seed=0):
    out = dict(first_inputs(seed))
    for name, value in second_inputs(seed + 1).items():
        if name != "x":
            out[name + "_2"] = value
    return out


def reference(
    x, attn_norm, mlp_norm, final_norm, swa_w_qkv, swa_sinks, swa_w_o, sb_w_qkv, sb_w_o,
    ret_w_in, ret_w_o, mlp_w_up, mlp_w_down, c_2, ctx_2, c_ctx_2, w_mod_2, b_mod_2, norm1_g_2,
    w_in_2, q_a_norm_g_2, kv_a_norm_g_2, w_q_up_2, w_kv_up_2, q_norm_g_2, k_norm_g_2,
    w_o_attn_2, w_fourier_2, w_out_2, norm2_g_2, w_router_2, w_e_gate_2, w_e_up_2, w_e_down_2,
):
    x = first_block(
        x, attn_norm, mlp_norm, final_norm, swa_w_qkv, swa_sinks, swa_w_o, sb_w_qkv, sb_w_o,
        ret_w_in, ret_w_o, mlp_w_up, mlp_w_down,
    )
    return second_block(
        x, c_2, ctx_2, c_ctx_2, w_mod_2, b_mod_2, norm1_g_2, w_in_2, q_a_norm_g_2,
        kv_a_norm_g_2, w_q_up_2, w_kv_up_2, q_norm_g_2, k_norm_g_2, w_o_attn_2, w_fourier_2,
        w_out_2, norm2_g_2, w_router_2, w_e_gate_2, w_e_up_2, w_e_down_2,
    )


_drawn_inputs = setup_inputs


def setup_inputs(seed=0):
    import zlib

    import numpy as np

    out = dict(_drawn_inputs(seed))
    spreads = {}
    factors = {'attn_norm': 5.4,
     'mlp_norm': 3.021,
     'final_norm': 2.885,
     'swa_sinks': 2.858,
     'ctx_2': 8.0,
     'c_ctx_2': 8.0,
     'b_mod_2': 4.457,
     'norm1_g_2': 8.0,
     'q_a_norm_g_2': 8.0,
     'kv_a_norm_g_2': 8.0,
     'w_q_up_2': 4.603,
     'q_norm_g_2': 8.0,
     'k_norm_g_2': 8.0,
     'norm2_g_2': 8.0}
    for name, (base, spread) in spreads.items():
        noise = np.random.default_rng([zlib.crc32(name.encode()), seed]).standard_normal(out[name].shape)
        drawn = base * np.exp(spread * noise) if base else spread * noise
        out[name] = __import__('jax').numpy.asarray(drawn.astype(out[name].dtype))
    for name, factor in factors.items():
        out[name] = (out[name] * factor).astype(out[name].dtype)
    return out
```

```python
from contextlib import ExitStack

import numpy as np

import concourse.bass as bass
from concourse import mybir

F32 = mybir.dt.float32
F32R = mybir.dt.float32r
U32 = mybir.dt.uint32
ALU = mybir.AluOpType
ACT = mybir.ActivationFunctionType
AX = mybir.AxisListType

P = 128
T = 1024
TC = 256
TA = T + TC
EPS = 1e-6
KB = 1024
MLA_SCALE = 96.0 ** -0.5

O_CONST = 0
O_RING = 7 * KB
N_RAW, N_HL = 3, 4
O_X = O_RING + N_RAW * 4 * KB + N_HL * 8 * KB
O_U = O_X + 32 * KB
O_V = O_U + 64 * KB
ARENA = O_V + 60 * KB


class Sem:

    def __init__(self, handle):
        self.handle, self.n = handle, 0


class Queue:

    def __init__(self, sem):
        self.ops, self.sem, self.waited = [], sem, {}

    def wait(self, *tokens):
        for t in tokens:
            if t is None:
                continue
            if isinstance(t, list):
                self.wait(*t)
                continue
            sem, value = t
            if self.waited.get(id(sem), 0) < value:
                self.waited[id(sem)] = value
                self.ops.append(("wait", sem, value))

    def do(self, fn, *tokens):
        self.wait(*tokens)
        self.sem.n += 1
        self.ops.append(("do", fn, self.sem, 1))
        return (self.sem, self.sem.n)

    def quiet(self, fn, *tokens):
        self.wait(*tokens)
        self.ops.append(("do", fn, None, 0))

    def mark(self):
        _, fn, sem, _ = self.ops[-1]
        if sem is not None:
            return (self.sem, self.sem.n)
        self.sem.n += 1
        self.ops[-1] = ("do", fn, self.sem, 1)
        return (self.sem, self.sem.n)

    def dma(self, fn, sem, *tokens):
        self.wait(*tokens)
        sem.n += 16
        self.ops.append(("do", fn, sem, 16))
        return (sem, sem.n)

    def emit(self, eng):
        for op in self.ops:
            if op[0] == "wait":
                eng.wait_ge(op[1].handle, op[2])
            else:
                ins = op[1](eng)
                if op[2] is not None:
                    ins.then_inc(op[2].handle, op[3])


def build(nc, A, out):
    ctx = ExitStack()
    with ctx:
        _program(nc, A, out, ctx)


def _program(nc, A, out, ctx):
    def sem(name):
        return Sem(ctx.enter_context(nc.semaphore(name)))

    pe, act, dve, pool, sp = (Queue(sem("s_" + n)) for n in ("pe", "act", "dve", "pool", "sp"))
    base = (nc.sbuf_base + 31) // 32 * 32
    ctx.enter_context(nc.sbuf_tensor("arena", [P, ARENA // 4], F32))
    psum = ctx.enter_context(nc.psum_tensor("psum", [P, 8, 512], F32))

    def at(name, shape, off, dt=F32):
        return nc.alloc_sbuf_tensor_at(name, [P] + list(shape), dt, offset=base + off)

    def pair(name, shape, off_hi, off_lo):
        return at(name + "_hi", shape, off_hi, F32R), at(name + "_lo", shape, off_lo, F32R)

    def f(ap):
        return ap.bitcast(F32)

    ident = at("ident", [128], O_CONST)
    ones = at("ones", [128], O_CONST + 512)
    vec = at("vec", [128], O_CONST + 1024)
    mod = at("mod", [64], O_CONST + 1536)
    gq = at("gq", [96], O_CONST + 2048)
    gk = at("gk", [96], O_CONST + 2048 + 384)
    rope = at("rope", [8, 64], O_CONST + 3072)
    small = at("small", [128], O_CONST + 5120)
    st = at("st", [4, 16], O_CONST + 5632)
    modb = at("modb", [64], O_CONST + 5888)
    G1, G2, GF = vec[:, 0:8], vec[:, 8:16], vec[:, 16:24]
    N1, N2 = vec[:, 24:32], vec[:, 32:40]
    GQA, GKVA = vec[:, 40:43], vec[:, 43:45]
    BMOD = vec[:, 48:96]
    SINK = vec[:, 96:112]
    EPSV = vec[:, 112:113]
    INV1024, INV384, INV256 = vec[:, 113:114], vec[:, 114:115], vec[:, 115:116]

    s_c = sem("s_const")
    c_tok = None
    for dst, src in ((ident, "ident"), (ones, "ones"), (vec, "vec"), (gq, "gq"), (gk, "gk"), (rope, "rope")):
        c_tok = pool.dma(lambda e, d=dst, s=src: e.dma_start(d[:], A[s]), s_c)
    for q in (pe, act, dve):
        q.wait(c_tok)

    raws = [(O_RING + i * 4 * KB) for i in range(N_RAW)]
    raw_t = [at(f"raw{i}", [1024], o) for i, o in enumerate(raws)]
    raw_s = [sem(f"s_raw{i}") for i in range(N_RAW)]
    hl = [pair(f"w{i}", [1024], O_RING + N_RAW * 4 * KB + i * 8 * KB, O_RING + N_RAW * 4 * KB + i * 8 * KB + 4 * KB)
          for i in range(N_HL)]

    class Stream:
        def __init__(self, raw, sems):
            self.raw, self.sems = raw, sems
            self.slot_free = [None] * len(raw)
            self.spec, self.loaded, self.parted, self.used = [], 0, 0, 0
            self.where, self.tok = {}, {}
            self.next_slot = 0
            self.hold = None
            self.ready, self.released = {}, {}
            self.pool_lo = False
            self.limit = 1 << 30

        def load(self):
            t = self.loaded
            name, i, width = self.spec[t]
            slot = self.next_slot % len(self.raw)
            self.next_slot += 1
            dst = self.raw[slot]
            self.where[t] = slot
            sp.wait(self.slot_free[slot])
            self.tok[t] = sp.dma(lambda e: e.dma_start(dst[:, 0:width], A[name][i]), self.sems[slot])
            self.loaded += 1

        def grow(self, raw, sems, free):
            keep = {self.where[t]: t for t in range(self.parted, self.loaded)}
            order = sorted(keep, key=lambda s: keep[s])
            idle = [s for s in range(len(self.raw)) if s not in keep]
            names = order + idle
            self.raw, old = [self.raw[s] for s in names] + raw, self.raw
            self.sems = [self.sems[s] for s in names] + sems
            self.slot_free = [self.slot_free[s] for s in names] + free
            for pos, s in enumerate(order):
                self.where[keep[s]] = pos
            self.next_slot = len(order)

        def part(self):
            t = self.parted
            width = self.spec[t][2]
            slot, (hi, lo) = self.where[t], hl[t % N_HL]
            raw = self.raw[slot]
            free = self.released.get(t - N_HL)
            h = act.do(lambda e: e.activation(hi[:, 0:width], raw[:, 0:width], ACT.Copy), self.tok[t], free)
            q = pool if self.pool_lo and t % 3 == 0 else dve
            l = q.do(lambda e: e.tensor_tensor(lo[:, 0:width], raw[:, 0:width], f(hi[:, 0:width]), ALU.subtract),
                     h, self.tok[t], free)
            self.ready[t] = [h, l]
            self.slot_free[slot] = [h, l]
            self.parted += 1

        def fill(self):
            while self.loaded < len(self.spec) and self.loaded < self.parted + len(self.raw):
                self.load()

        def take(self, ahead=None):
            t = self.used
            self.used += 1
            upto = t + (N_HL - 1 if ahead is None else ahead)
            self.fill()
            while self.parted < min(len(self.spec), self.limit) and self.parted <= upto and (
                    self.parted < N_HL or self.parted - N_HL in self.released):
                self.part()
                self.fill()
            assert self.parted > t
            hi, lo = hl[t % N_HL]
            return hi, lo, self.ready[t], t

        def release(self, t, token):
            self.released[t] = token

        def resume(self, *tokens):
            self.limit = 1 << 30
            for t in range(self.used - N_HL, self.used):
                self.released[t] = list(tokens)

    W = Stream(raw_t, raw_s)

    def plan(name, n, width=1024):
        for i in range(n):
            W.spec.append((name, i, width))

    plan("w_k", 1)
    plan("w_v", 1)
    plan("w_q", 8)
    plan("w_so", 8)
    W.spec += [("w_up", i, 1024) for i in range(6)]
    for g in range(8):
        W.spec += [("w_dn", 4 * g + i, 1024) for i in range(4)]
        W.spec += [("w_up", i, 1024) for i in range(4 * g + 6, min(4 * g + 10, 32))]
    plan("w_f", 4)
    plan("dft_t", 16)
    for j in range(8):
        W.spec.append(("w_gb", j, 1024))
        if j % 2 == 0:
            W.spec.append(("w_fo", j // 2, 1024))
    plan("w_qa", 3)
    plan("w_kva", 2)
    plan("w_kpe", 1, 256)
    W.spec += [("w_ga", j, 1024) for j in range(3)]
    plan("w_qup", 3, 768)
    plan("w_kup", 1)
    W.spec += [("w_ga", j, 1024) for j in range(3, 8)]
    plan("w_vup", 1)
    W.limit = len(W.spec)
    plan("w_ao", 4)
    plan("w_out", 8)
    plan("w_e", 192)

    free = [None] * 8
    turn = [0]
    held = set()

    def banks(n=1):
        b = turn[0]
        while b + n > 8 or held & set(range(b, b + n)):
            b = (b + 1) % 8
        turn[0] = (b + n) % 8
        for i in range(b, b + n):
            pe.wait(free[i])
            free[i] = None
        return b

    def done(b, n, *tokens):
        for i in range(b, b + n):
            free[i] = list(tokens)

    def bank(b, lo=0, hi=512, n=1):
        return psum[:, b, lo:hi] if n == 1 else psum[:, b:b + n, :].rearrange("p b n -> p (b n)")[:, lo:hi]

    def mm(o, l, r, start, stop, tokens=(), skip=False):
        pe.quiet(lambda e: e.matmul(o, l, r, start=start, stop=stop, skip_group_check=skip), *tokens)

    def mm3(o, l, r, first, last, tokens=()):
        mm(o, l[0], r[0], first, False, tokens)
        mm(o, l[1], r[0], False, False)
        mm(o, l[0], r[1], False, last)

    def part(src, hi, lo, tokens, free_tok=None, bias=None, q=None):
        if bias is None:
            h = act.do(lambda e: e.activation(hi, src, ACT.Copy), tokens, free_tok)
            l = (q or dve).do(lambda e: e.tensor_tensor(lo, src, f(hi), ALU.subtract), tokens, h, free_tok)
        else:
            h = act.do(lambda e: e.activation(hi, src, ACT.Identity, bias=bias), tokens, free_tok)
            l = dve.do(lambda e: e.scalar_tensor_tensor(lo, src, bias, f(hi), ALU.add, ALU.subtract),
                       tokens, h, free_tok)
        return [h, l]

    class Norm:

        def __init__(self, inv, width, sq, tokens_sq=None):
            self.b, self.inv, self.w, self.nb = banks(1), inv, width, width // P
            self.sq, self.sqf, self.k = sq, [tokens_sq] * len(sq), 0
            held.add(self.b)

        def add(self, x, *tokens, last=False):
            sq = self.sq[self.k % len(self.sq)]
            t = act.do(lambda e: e.activation(sq[:, 0:self.w], x, ACT.Square), *tokens, self.sqf[self.k % len(self.sq)])
            for tb in range(self.nb):
                mm(psum[:, self.b, tb:tb + 1], sq[:, tb * P:(tb + 1) * P], self.inv,
                   self.k == 0 and tb == 0, last and tb == self.nb - 1, (t,), True)
            self.m = pe.mark()
            self.sqf[self.k % len(self.sq)] = self.m
            self.k += 1

        def finish(self, dg, dg_free, s):
            nb = self.nb
            sd, r = st[:, s, 0:nb], st[:, s + 1, 0:nb]
            a = act.do(lambda e: e.activation(sd, psum[:, self.b, 0:nb], ACT.Sqrt, bias=EPSV), self.m, rs_free[0])
            done(self.b, 1, a)
            held.discard(self.b)
            v = dve.do(lambda e: e.reciprocal(r, sd), a, rs_free[0])
            d = dve.do(lambda e: e.tensor_tensor(
                dg[:, 0:nb, :], ident[:, None, :].to_broadcast([P, nb, P]),
                r.unsqueeze(2).to_broadcast([P, nb, P]), ALU.mult), v, dg_free)
            n = (nb + 3) // 4
            b = banks(n)
            for i in range(n):
                w = min(4, nb - 4 * i)
                mm(psum[:, b + i, 0:w * P], ones[:], dg[:, 4 * i:4 * i + w, :].rearrange("p a b -> p (a b)"),
                   True, True, (d,))
            rs_free[0] = [d]
            self.dg_done = pe.mark()
            return b, n, self.dg_done

    rs_free = [None]

    def two(b, c0=0, c1=1024):
        return psum[:, b:b + 2, :].rearrange("p b n -> p (b n)")[:, c0:c1]

    def finish_program(last_tokens):
        sp.wait(*last_tokens, *[(x, x.n) for x in W.sems])
        with nc.Block() as block:
            @block.sync
            def _(e):
                sp.emit(e)

            @block.gpsimd
            def _(e):
                pool.emit(e)

            @block.scalar
            def _(e):
                act.emit(e)

            @block.vector
            def _(e):
                dve.emit(e)

            @block.tensor
            def _(e):
                pe.emit(e)


    X = at("X", [8, 1024], O_X)
    s_x = [sem(f"s_x{i}") for i in range(4)]
    x_tok = [None] * 8
    for i in range(4):
        t = sp.dma(lambda e, i=i: e.dma_start(X[:, 2 * i:2 * i + 2, :], A["xT"][:, 2 * i:2 * i + 2, :]), s_x[i])
        x_tok[2 * i] = x_tok[2 * i + 1] = t
    W.fill()

    sq = [at(f"sq{i}", [1024], O_V + (48 + 4 * i) * KB) for i in range(2)]
    dg = at("dg", [8, P], O_V + 56 * KB)
    tmp = [at(f"tmp{i}", [1024], O_V + 4 * i * KB) for i in range(2)]
    tmp_free = [None, None]
    U = pair("U", [8, 1024], O_U, O_U + 32 * KB)

    def apply_norm(rb, rtok, gain, k, x, dst, xtok, dst_free, shift=None, width=1024):
        tb = tmp[k % 2]
        r = psum[:, rb:rb + 2, :].rearrange("p b n -> p (b n)")[:, 0:width]
        a = dve.do(lambda e: e.scalar_tensor_tensor(tb[:, 0:width], x, gain, r, ALU.mult, ALU.mult),
                   xtok, rtok, tmp_free[k % 2])
        toks = part(tb[:, 0:width], dst[0], dst[1], a, dst_free, bias=shift)
        tmp_free[k % 2] = toks
        return toks, a

    nm = Norm(INV1024, T, sq)
    for k in range(8):
        nm.add(X[:, k, :], x_tok[k], last=k == 7)
    rb, rn, rtok = nm.finish(dg, None, 0)
    u_tok = [None] * 8
    for k in range(8):
        u_tok[k], a = apply_norm(rb, rtok, G1[:, k:k + 1], k, X[:, k, :], (U[0][:, k, :], U[1][:, k, :]),
                                 x_tok[k], None)
    done(rb, rn, a)
    x_dead = a

    def ch(t, k, c0=0, c1=1024):
        return (t[0][:, k, c0:c1], t[1][:, k, c0:c1])

    def wt(tile, kc, n):
        return tile[0][:, kc * n:(kc + 1) * n], tile[1][:, kc * n:(kc + 1) * n]

    def proj_T(act_t, toks, nk=8, halves=((0, 512), (512, 1024)), base_k=0, n_w=128, sub=0, tile=None):
        res = []
        own = tile is None
        if own:
            tile = W.take()
        for c0, c1 in halves:
            b = banks(1)
            for k in range(nk):
                l = (tile[0][:, k * n_w + sub:k * n_w + sub + 128], tile[1][:, k * n_w + sub:k * n_w + sub + 128])
                mm3(psum[:, b, 0:c1 - c0], l, ch(act_t, k, c0, c1), k == 0, k == nk - 1, (tile[2], toks[k]))
            res.append((b, pe.mark()))
        if own:
            W.release(tile[3], res[-1][1])
        return res

    qb_ = [pair(f"q{i}", [1024], O_V + 8 * i * KB, O_V + (8 * i + 4) * KB) for i in range(2)]
    kT = pair("kT", [1024], O_V + 16 * KB, O_V + 20 * KB)
    vz = pair("vz", [8, 192], O_V + 24 * KB, O_V + 30 * KB)
    bias = [at(f"bias{i}", [2, 256], O_X + (24 + 2 * i) * KB) for i in range(2)]
    L = [at(f"L{i}", [8, 256], O_X + 8 * i * KB) for i in range(2)]
    pt = [pair(f"pt{i}", [512], O_X + (16 + 4 * i) * KB, O_X + (18 + 4 * i) * KB) for i in range(2)]
    oraw = [at(f"oraw{j}", [1024], O_V + (36 + 4 * j) * KB) for j in range(6)]

    kt_tok = []
    tmpk = L[0][:, 0:4, :].rearrange("p a b -> p (a b)")
    for i, (b, m) in enumerate(proj_T(U, u_tok)):
        c = dve.do(lambda e, b=b, i=i: e.tensor_scalar(tmpk[:, 512 * i:512 * i + 512], bank(b), 0.125, None, ALU.mult),
                   m, x_dead)
        done(b, 1, c)
        kt_tok += part(tmpk[:, 512 * i:512 * i + 512], kT[0][:, 512 * i:512 * i + 512],
                       kT[1][:, 512 * i:512 * i + 512], c, tmp_free)
    z = vz[0][:].rearrange("p a b -> p (a b)"), vz[1][:].rearrange("p a b -> p (a b)")
    zt = [dve.do(lambda e, x=x: e.memset(f(x), 0.0)) for x in z]
    vt = W.take()
    v_tok = []
    for q4 in range(2):
        b = banks(1)
        for n in range(4):
            tb = 4 * q4 + n
            for k in range(8):
                mm3(psum[:, b, n * P:(n + 1) * P], ch(U, k, tb * P, tb * P + P), wt(vt, k, 128),
                    k == 0, k == 7, (vt[2],))
        m = pe.mark()
        src = psum[:, b, :].rearrange("p (n h d) -> p n h d", n=4, h=2)
        d0, d1 = (vz[i][:, 4 * q4:4 * q4 + 4, :].rearrange("p n (a d) -> p n a d", d=64)[:, :, 0:3:2, :]
                  for i in range(2))
        hs = part(src, d0, d1, m, zt)
        v_tok += hs
        done(b, 1, *hs)
    W.release(vt[3], m)

    s_bias = [sem(f"s_bias{i}") for i in range(2)]
    bias_free = [x_dead, x_dead]
    bias_tok = [None, None]
    L_free = [[x_dead, kt_tok], [x_dead, kt_tok]]
    pt_free = [x_dead, x_dead]
    q_free = [tmp_free, None]
    q_tok = [None, None]
    oraw_tok = {}
    ucur = [None]
    small_free = [None]
    negm = small[:, 0:32].rearrange("p (b x) -> p b x", b=2)
    rsum = small[:, 32:64].rearrange("p (b x) -> p b x", b=2)
    sexp = small[:, 64:96].rearrange("p (b x) -> p b x", b=2)
    sm_free = [None, None]
    O1 = U
    o_tok = [None] * 8

    def load_bias(j):
        bias_tok[j % 2] = pool.dma(lambda e: e.dma_start(bias[j % 2][:], A["bias"][j]), s_bias[j % 2], bias_free[j % 2])

    def q_proj(j):
        toks = []
        for i, (b, m) in enumerate(proj_T(U, u_tok)):
            sl = slice(512 * i, 512 * i + 512)
            p = part(bank(b), qb_[j % 2][0][:, sl], qb_[j % 2][1][:, sl], m, q_free[j % 2])
            done(b, 1, *p)
            toks += p
        q_tok[j % 2] = toks
        return m

    sinkc = [None]

    def scores(j, hf):
        s = (2 * j + hf) % 2
        q = qb_[j % 2]
        Lt, toks, mx = L[s], [], negm[:, s, :]
        if hf == 0:
            load_bias(j)
        for n2 in range(2):
            b = banks(2)
            for n4 in (2 * n2, 2 * n2 + 1):
                n = 4 * hf + n4
                lo = 0 if n == 0 else (n - 1) * P
                w = (n + 1) * P - lo
                c1 = 256 * (n4 % 2) + 256
                for x, y in ((0, 0), (1, 0), (0, 1)):
                    for h in range(2):
                        pr = slice(64 * h, 64 * h + 64)
                        mm(psum[:, b + h, c1 - w:c1], q[x][pr, n * P:(n + 1) * P], kT[y][pr, lo:lo + w],
                           (x, y) == (0, 0), (x, y) == (0, 1), (q_tok[j % 2], kt_tok))
            m = pe.mark()
            for h in range(2):
                for n4 in (2 * n2, 2 * n2 + 1):
                    w = 128 if hf == 0 and n4 == 0 else 256
                    c1, i = 256 * (n4 % 2) + 256, 2 * n4 + h
                    d = dve.do(lambda e, b=b, h=h, i=i, w=w, c1=c1: e.tensor_tensor_reduce(
                        Lt[:, i, 256 - w:256], psum[:, b + h, c1 - w:c1],
                        bias[j % 2][:, h, 256 - w:256], 1.0, -3.0e38, ALU.add, ALU.max, mx[:, i:i + 1]),
                        m, bias_tok[j % 2], L_free[s], sm_free[s])
                done(b + h, 1, d)
            toks.append(d)
        if hf == 1:
            bias_free[j % 2] = toks[-1]
        mv = mx[:, 0:8].rearrange("p (n h) -> p n h", h=2)
        sk = SINK[:, 2 * j:2 * j + 2].unsqueeze(1).to_broadcast([P, 4, 2])
        nm_ = mx[:, 8:16].rearrange("p (n h) -> p n h", h=2)
        sx = sexp[:, s, 0:8].rearrange("p (n h) -> p n h", h=2)
        a = dve.do(lambda e: e.tensor_tensor(nm_, mv, sk, ALU.max), toks[-1], sm_free[s])
        a2 = dve.do(lambda e: e.tensor_scalar(mx[:, 0:8], mx[:, 8:16], -1.0, None, ALU.mult), a)
        a3 = dve.do(lambda e: e.tensor_tensor(sx, sk, nm_, ALU.subtract), a, sm_free[s])
        es = act.do(lambda e: e.activation(sexp[:, s, 8:16], sexp[:, s, 0:8], ACT.Exp), a3, sm_free[s])
        ex = []
        for i in range(8):
            w = 128 if (hf == 0 and i < 2) else 256
            ex.append(act.do(lambda e, i=i, w=w: e.activation(
                Lt[:, i, 256 - w:256], Lt[:, i, 256 - w:256], ACT.Exp, bias=mx[:, i:i + 1],
                accum_out=rsum[:, s, i:i + 1]), a2, sm_free[s]))
        d = dve.do(lambda e: e.tensor_tensor(rsum[:, s, 8:16], rsum[:, s, 0:8], sexp[:, s, 8:16], ALU.add), ex[-1], es)
        r_ = dve.do(lambda e: e.reciprocal(rsum[:, s, 0:8], rsum[:, s, 8:16]), d)
        ns = []
        for i in range(8):
            w = 128 if (hf == 0 and i < 2) else 256
            ns.append(dve.do(lambda e, i=i, w=w: e.tensor_scalar(
                Lt[:, i, 256 - w:256], Lt[:, i, 256 - w:256], rsum[:, s, i:i + 1], None, ALU.mult), r_, ex[i]))
        sm_free[s] = ns[-1]
        return ns

    def values(j, hf, ns):
        s = (2 * j + hf) % 2
        Lt = L[s]
        ob = banks(1)
        for n4 in range(4):
            n = 4 * hf + n4
            kbs = (1,) if n == 0 else (0, 1)
            b = banks(1)
            p_ = pt[n4 % 2]
            for h in range(2):
                for kb in kbs:
                    o = psum[:, b, (2 * h + kb) * P:(2 * h + kb + 1) * P]
                    src = Lt[:, 2 * n4 + h, kb * P:(kb + 1) * P]
                    pe.quiet(lambda e, o=o, src=src: e.transpose(o, src, ident[:]), ns[2 * n4 + h])
            m = pe.mark()
            if n4 == 3:
                L_free[s] = m
            v = lambda x: x.rearrange("p (h k q) -> p h k q", h=2, k=2)[:, :, kbs[0]:2, :]
            pp = part(v(psum[:, b, :]), v(p_[0][:]), v(p_[1][:]), m, pt_free[n4 % 2])
            done(b, 1, *pp)
            first = True
            for h in range(2):
                for kb in kbs:
                    l = [vz[i][:, n - 1 + kb, 64 * h:64 * h + 128] for i in range(2)]
                    r = [p_[i][:, (2 * h + kb) * P:(2 * h + kb + 1) * P] for i in range(2)]
                    mm3(psum[:, ob, n4 * P:(n4 + 1) * P], l, r, first, h == 1 and kb == 1, (pp, v_tok))
                    first = False
            pt_free[n4 % 2] = pe.mark()
        m = pt_free[1]
        sl = slice(512 * hf, 512 * hf + 512)
        if j < 6:
            t = act.do(lambda e: e.activation(oraw[j][:, sl], bank(ob), ACT.Copy), m, nm.dg_done)
            oraw_tok.setdefault(j, []).append(t)
            done(ob, 1, t)
        else:
            t = part(bank(ob), O1[0][:, j, sl], O1[1][:, j, sl], m, ucur[0])
            o_tok[j] = (o_tok[j] or []) + t
            done(ob, 1, *t)
        return m

    q_proj(0)
    pend = None
    for j in range(8):
        if j < 7:
            last_u = q_proj(j + 1)
            if j == 6:
                ucur[0] = last_u
        for hf in range(2):
            ns = scores(j, hf)
            if pend is not None:
                m = values(*pend)
                if pend[1] == 1:
                    q_free[pend[0] % 2] = m
            pend = (j, hf, ns)
        if j == 6:
            for i in range(6):
                o_tok[i] = part(oraw[i][:], O1[0][:, i, :], O1[1][:, i, :], oraw_tok[i], ucur[0])
    m_att = values(*pend)
    osplit = [t for i in range(6) for t in o_tok[i]]

    s_x2 = [sem(f"s_xr{i}") for i in range(4)]
    for i in range(4):
        t = pool.dma(lambda e, i=i: e.dma_start(X[:, 2 * i:2 * i + 2, :], A["xT"][:, 2 * i:2 * i + 2, :]),
                     s_x2[i], m_att, bias_free, L_free)
        x_tok[2 * i] = x_tok[2 * i + 1] = t

    nm = Norm(INV1024, T, sq, osplit)
    for n in range(8):
        res = proj_T(O1, o_tok)
        ts = []
        for i, (b, m) in enumerate(res):
            sl = slice(512 * i, 512 * i + 512)
            t = dve.do(lambda e, b=b, sl=sl, n=n: e.tensor_tensor(X[:, n, sl], bank(b), X[:, n, sl], ALU.add),
                       m, x_tok[n])
            done(b, 1, t)
            ts.append(t)
        x_tok[n] = ts
        nm.add(X[:, n, :], ts, last=n == 7)
    u_dead = m
    rb, rn, rtok = nm.finish(dg, osplit, 0)
    for k in range(8):
        tmp_free[k % 2] = tmp_free[k % 2] if k > 1 else [tmp_free[k % 2], m_att]
        u_tok[k], a = apply_norm(rb, rtok, G2[:, k:k + 1], k, X[:, k, :], ch(U, k), x_tok[k], u_dead)
    done(rb, rn, a)

    NA = 6
    ab = [pair(f"a{i}", [1024], O_V + 8 * i * KB, O_V + (8 * i + 4) * KB) for i in range(NA)]
    a_free = [[u_tok, m_att] for _ in range(NA)]
    a_tok = {}
    relu = [at(f"relu{i}", [512], O_V + (56 + 2 * i) * KB) for i in range(2)]
    r_free = [nm.dg_done, nm.dg_done]
    ri = [0]
    mraw = [at(f"mraw{i}", [512], O_V + (48 + 2 * i) * KB) for i in range(2)]
    srow = at("srow", [1024], O_V + 52 * KB)
    s_m = [sem(f"s_m{i}") for i in range(2)]
    m_free = [nm.sqf, nm.sqf]
    s_s = sem("s_srow")
    s_state = {"tok": None, "free": nm.sqf}
    mod_jobs = [(0, i) for i in range(96)] + [(1, i) for i in range(32)]
    mod_ld = {}

    def silu_row(name):
        t = pool.dma(lambda e: e.dma_start(srow[:], A[name]), s_s, s_state["free"])
        s_state["tok"] = act.do(lambda e: e.activation(srow[:], srow[:], ACT.Silu), t)

    def mod_load(n):
        if n < 128:
            i = mod_jobs[n][1]
            mod_ld[n] = pool.dma(lambda e: e.dma_start(mraw[n % 2][:], A["w_mod"][i]), s_m[n % 2], m_free[n % 2])

    def mod_step(n):
        who, i = mod_jobs[n]
        if n == 0:
            mod_load(0)
            mod_load(1)
            silu_row("c_b")
        if n == 96:
            silu_row("cc_b")
        c = 48 * who + i // 2
        dst = (modb if i % 2 else mod)[:, c:c + 1]
        t = dve.do(lambda e: e.tensor_tensor_reduce(mraw[n % 2][:], mraw[n % 2][:],
                                                    srow[:, 512 * (i % 2):512 * (i % 2) + 512], 1.0, 0.0,
                                                    ALU.mult, ALU.add, dst),
                   mod_ld[n], s_state["tok"])
        m_free[n % 2] = t
        s_state["free"] = t
        mod_load(n + 2)

    def up(i):
        s = i % NA
        toks = []
        for hfi, (b, m) in enumerate(proj_T(U, u_tok)):
            sl = slice(512 * hfi, 512 * hfi + 512)
            rr, rf = relu[ri[0] % 2], ri[0] % 2
            ri[0] += 1
            t1 = act.do(lambda e, rr=rr, b=b: e.activation(rr[:], bank(b), ACT.Relu), m, r_free[rf])
            done(b, 1, t1)
            t2 = act.do(lambda e, rr=rr, s=s, sl=sl: e.activation(ab[s][0][:, sl], rr[:], ACT.Square), t1, a_free[s])
            t3 = dve.do(lambda e, rr=rr: e.tensor_tensor(rr[:], rr[:], rr[:], ALU.mult), t1, t2)
            t4 = dve.do(lambda e, rr=rr, s=s, sl=sl: e.tensor_tensor(
                ab[s][1][:, sl], rr[:], f(ab[s][0][:, sl]), ALU.subtract), t2, t3, a_free[s])
            r_free[rf] = t4
            toks += [t2, t4]
        a_tok[i] = toks

    def down(g, last, nm=None):
        for q4 in range(4):
            tile = W.take()
            for n in (2 * q4, 2 * q4 + 1):
                ts = []
                for hfi in range(2):
                    b = banks(1)
                    for c in range(4):
                        i = 4 * g + c
                        l = [tile[x][:, c * 256 + (n % 2) * 128:c * 256 + (n % 2) * 128 + 128] for x in range(2)]
                        r = [ab[i % NA][x][:, 512 * hfi:512 * hfi + 512] for x in range(2)]
                        mm3(psum[:, b, :], l, r, c == 0, c == 3, (tile[2], a_tok[i]))
                    m = pe.mark()
                    sl = slice(512 * hfi, 512 * hfi + 512)
                    t = dve.do(lambda e, b=b, n=n, sl=sl: e.tensor_tensor(
                        X[:, n, sl], bank(b), X[:, n, sl], ALU.add), m, x_tok[n], u_tok)
                    done(b, 1, t)
                    ts.append(t)
                x_tok[n] = ts
                if last:
                    nm.add(X[:, n, :], ts, last=n == 7)
            W.release(tile[3], m)
        for c in range(4):
            a_free[(4 * g + c) % NA] = m

    nx, jobs = 0, 0

    def ups(n):
        nonlocal nx, jobs
        for _ in range(n):
            if nx < 32:
                up(nx)
                nx += 1
                if nx >= 2:
                    for _ in range(5):
                        if jobs < 128:
                            mod_step(jobs)
                            jobs += 1
    ups(6)
    for g in range(8):
        last = g == 7
        if last:
            assert jobs == 128
            nm = Norm(INV1024, T, sq, [m_free, s_state["free"]])
        down(g, last, nm)
        ups(4)
    m0 = dve.do(lambda e: e.tensor_tensor(mod[:], mod[:], modb[:], ALU.add), m_free)
    mt = dve.do(lambda e: e.tensor_tensor(mod[:, 0:48], mod[:, 0:48], BMOD, ALU.add), m0)
    mt2 = dve.do(lambda e: e.tensor_tensor(mod[:, 48:64], mod[:, 48:64], BMOD[:, 0:16], ALU.add), m0)
    t1 = dve.do(lambda e: e.scalar_tensor_tensor(mod[:, 8:16], mod[:, 8:16], 1.0, N1, ALU.add, ALU.mult), mt)
    t2 = dve.do(lambda e: e.scalar_tensor_tensor(mod[:, 32:40], mod[:, 32:40], 1.0, N2, ALU.add, ALU.mult), mt)
    t3 = dve.do(lambda e: e.scalar_tensor_tensor(mod[:, 56:64], mod[:, 56:64], 1.0, N1, ALU.add, ALU.mult), mt2)
    mod_tok = [t1, t2, t3]
    SH1, SC1, GT1 = mod[:, 0:8], mod[:, 8:16], mod[:, 16:24]
    SH2, SC2, GT2 = mod[:, 24:32], mod[:, 32:40], mod[:, 40:48]
    CSH1, CSC1 = mod[:, 48:56], mod[:, 56:64]

    rb, rn, rtok = nm.finish(dg, [r_free, nm.sqf], 0)
    nm2 = Norm(INV1024, T, sq, nm.sqf)
    s_sp = sem("s_spill")
    for k in range(8):
        t = dve.do(lambda e, k=k, r=two(rb): e.scalar_tensor_tensor(
            X[:, k, :], X[:, k, :], GF[:, k:k + 1], r, ALU.mult, ALU.mult), rtok, x_tok[k])
        x_tok[k] = t
        nm2.add(X[:, k, :], t, last=k == 7)
        spilled = pool.dma(lambda e, k=k: e.dma_start(A["x1s"][:, k, :], X[:, k, :]), s_sp, t)
    done(rb, rn, t)
    a_dead = m
    rb, rn, rtok = nm2.finish(dg, nm.dg_done, 2)
    tmp_free = [a_dead, a_dead]
    for k in range(8):
        u_tok[k], a = apply_norm(rb, rtok, SC1[:, k:k + 1], k, X[:, k, :], ch(U, k), [x_tok[k], mod_tok], a_dead,
                                 shift=SH1[:, k:k + 1])
    done(rb, rn, a)
    x1_dead = [a, spilled, nm2.m]
    fT = pair("fT", [1024], O_V, O_V + 4 * KB)
    Zh = at("Z_hi", [4, 8, 256], O_X, F32R)
    Zl = at("Z_lo", [4, 8, 256], O_V + 8 * KB, F32R)
    cdr = at("cdr", [256], O_V + 42 * KB)
    cdp = pair("cd", [256], O_V + 40 * KB, O_V + 41 * KB)
    s_cd = sem("s_cd")
    t = pool.dma(lambda e: e.dma_start(cdr[:], A["dft_c"]), s_cd, a_dead)
    cd = (cdp[0], cdp[1], part(cdr[:], cdp[0][:], cdp[1][:], t, a_dead))
    f_free = tmp_free
    for g in range(4):
        ft = []
        for i, (b, m) in enumerate(proj_T(U, u_tok)):
            sl = slice(512 * i, 512 * i + 512)
            p = part(bank(b), fT[0][:, sl], fT[1][:, sl], m, f_free)
            done(b, 1, *p)
            ft.append(p)
        for n2 in range(4):
            b = banks(1)
            for i in range(2):
                n = 2 * n2 + i
                l = (fT[0][:, n * P:n * P + P], fT[1][:, n * P:n * P + P])
                mm3(psum[:, b, 256 * i:256 * i + 256], l, (cd[0][:, 0:256], cd[1][:, 0:256]),
                    True, True, (ft[n // 4], cd[2]))
            m = pe.mark()
            z0, z1 = (z[:, g, 2 * n2:2 * n2 + 2, :].rearrange("p a b -> p (a b)") for z in (Zh, Zl))
            p = part(bank(b), z0, z1, m, [x1_dead, a_dead])
            done(b, 1, *p)
            z_tok = p
        f_free = m
    turn[0] = 0
    banks(8)
    for c in range(16):
        tile = W.take()
        for g in range(4):
            n, cs = c % 8, c // 8
            l = tuple(z[:, g, n, 128 * cs:128 * cs + 128] for z in (Zh, Zl))
            for i in range(2):
                r = (tile[0][:, 512 * i:512 * i + 512], tile[1][:, 512 * i:512 * i + 512])
                mm3(psum[:, 2 * g + i, :], l, r, c == 0, c == 15, (tile[2], z_tok))
        m = pe.mark()
        W.release(tile[3], m)
    z_dead = m
    Y = pair("Y", [4, 1024], O_X, O_X + 16 * KB)
    y_tok = []
    for g in range(4):
        yt = []
        for i in range(2):
            sl = slice(512 * i, 512 * i + 512)
            p = part(bank(2 * g + i), Y[0][:, g, sl], Y[1][:, g, sl], m)
            done(2 * g + i, 1, *p)
            yt += p
        y_tok.append(yt)
    cT = at("cT", [8, 256], O_V + 8 * KB)
    HC = pair("HC", [8, 256], O_V + 16 * KB, O_V + 24 * KB)
    csq = [at(f"csq{i}", [256], O_V + (32 + i) * KB) for i in range(2)]
    ctmp = [at(f"ctmp{i}", [256], O_V + (34 + i) * KB) for i in range(2)]
    cdg = at("cdg", [2, P], O_V + 36 * KB)
    s_ct = sem("s_ctx")
    ct_tok = pool.dma(lambda e: e.dma_start(cT[:], A["ctxT"]), s_ct, z_dead)
    gbs = [at(f"gb{i}", [1024], O_V + (40 + 4 * i) * KB) for i in range(2)]
    tsb = [at(f"tsb{i}", [1024], O_V + (48 + 4 * i) * KB) for i in range(2)]
    s_ts = [sem(f"s_ts{i}") for i in range(2)]
    g_free, t_free = [nm2.sqf, nm2.sqf], [nm2.sqf, nm2.dg_done]
    hc_tok = [None] * 8
    ctx_end = []

    def context():
        cn = Norm(INV1024, TC, csq, z_dead)
        for k in range(8):
            cn.add(cT[:, k, :], ct_tok, last=k == 7)
        rb, rn, rtok = cn.finish(cdg, z_dead, 0)
        fr = [z_dead, z_dead]
        for k in range(8):
            a = dve.do(lambda e, k=k, r=bank(rb, 0, 256): e.scalar_tensor_tensor(
                ctmp[k % 2][:], cT[:, k, :], CSC1[:, k:k + 1], r, ALU.mult, ALU.mult), rtok, ct_tok, mod_tok, fr[k % 2])
            hc_tok[k] = part(ctmp[k % 2][:], HC[0][:, k, :], HC[1][:, k, :], a, z_dead, bias=CSH1[:, k:k + 1])
            fr[k % 2] = hc_tok[k]
        done(rb, rn, a)
        ctx_end.append([fr, cn.sqf, cn.dg_done])

    for j in range(8):
        if j == 1:
            context()
        gt, tt = gbs[j % 2], tsb[j % 2]
        ga_ = []
        for i, (b, m) in enumerate(proj_T(U, u_tok)):
            sl = slice(512 * i, 512 * i + 512)
            t = act.do(lambda e, b=b, sl=sl, gt=gt: e.activation(gt[:, sl], bank(b), ACT.Sigmoid), m, g_free[j % 2])
            done(b, 1, t)
            ga_.append(t)
        if j % 2 == 0:
            fo_tile = W.take()
        for i, (b, m) in enumerate(proj_T(Y, y_tok, nk=4, n_w=256, sub=128 * (j % 2), tile=fo_tile)):
            sl = slice(512 * i, 512 * i + 512)
            t = dve.do(lambda e, b=b, sl=sl, gt=gt, tt=tt: e.tensor_tensor(tt[:, sl], bank(b), gt[:, sl], ALU.mult),
                       m, ga_, t_free[j % 2])
            done(b, 1, t)
        if j % 2 == 1:
            W.release(fo_tile[3], m)
        g_free[j % 2] = t
        t_free[j % 2] = pool.dma(lambda e, j=j, tt=tt: e.dma_start(A["ts"][j], tt[:]), s_ts[j % 2], t)
    y_dead = m

    cqr = at("cqr", [3, 1024], O_X)
    ckr = at("ckr", [2, TA], O_X + 12 * KB)
    kpe = at("kpe", [10, 32], O_X + 30 * KB)
    cq = pair("cq", [3, 1024], O_V + 32 * KB, O_V + 44 * KB)
    ck = pair("ck", [2, TA], O_V + 8 * KB, O_V + 18 * KB)
    sq3 = [at(f"sq3_{i}", [1024], O_X + (22 + 4 * i) * KB) for i in range(2)]
    dg3 = at("dg3", [8, P], O_V + 28 * KB)
    gas = [at("gas0", [1024], O_X + 24 * KB), at("gas1", [1024], O_V + 56 * KB),
           at("gas2", [1024], O_V), at("gas3", [1024], O_V + 4 * KB)]
    s_ga = [sem(f"s_ga{i}") for i in range(4)]
    ga_free = [None] * 4

    n_q = Norm(INV384, T, sq3, y_dead)
    for k in range(3):
        ts = []
        for i, (b, m) in enumerate(proj_T(U, u_tok)):
            sl = slice(512 * i, 512 * i + 512)
            t = dve.do(lambda e, b=b, k=k, sl=sl: e.tensor_copy(cqr[:, k, sl], bank(b)), m, y_dead)
            done(b, 1, t)
            ts.append(t)
        n_q.add(cqr[:, k, :], ts, last=k == 2)
    cq_t = ts
    n_k = Norm(INV256, T, [sq3[0]], n_q.sqf)
    n_c = Norm(INV256, TC, [sq3[1]], n_q.sqf)
    for k in range(2):
        ts = []
        tile = W.take()
        res = proj_T(U, u_tok, tile=tile) + proj_T(HC, hc_tok, halves=((0, 256),), tile=tile)
        W.release(tile[3], res[-1][1])
        for i, (b, m) in enumerate(res):
            w = 512 if i < 2 else 256
            t = dve.do(lambda e, b=b, k=k, i=i, w=w: e.tensor_copy(ckr[:, k, 512 * i:512 * i + w], bank(b, 0, w)),
                       m, y_dead)
            done(b, 1, t)
            ts.append(t)
        n_k.add(ckr[:, k, 0:T], ts, last=k == 1)
        n_c.add(ckr[:, k, T:TA], ts, last=k == 1)
    ck_t = ts
    tile = W.take()
    b = banks(1)
    for n in range(10):
        src, c0 = (U, n * P) if n < 8 else (HC, (n - 8) * P)
        for k in range(8):
            mm3(psum[:, b, 32 * n:32 * n + 32], ch(src, k, c0, c0 + P), wt(tile, k, 32), k == 0, k == 7,
                (tile[2], hc_tok))
    hc_dead = pe.mark()
    W.release(tile[3], hc_dead)
    kpe_tok = dve.do(lambda e, b=b: e.tensor_copy(kpe[:].rearrange("p a b -> p (a b)"), bank(b, 0, 320)),
                     hc_dead, y_dead)
    done(b, 1, kpe_tok)

    def ga_block(j):
        s = j % 2 if j < 3 else 2 + j % 2
        gt = gas[s]
        for i, (b, m) in enumerate(proj_T(U, u_tok)):
            sl = slice(512 * i, 512 * i + 512)
            t = act.do(lambda e, b=b, sl=sl: e.activation(gt[:, sl], bank(b), ACT.Sigmoid), m, ga_free[s])
            done(b, 1, t)
        ga_free[s] = pool.dma(lambda e: e.dma_start(A["gas"][j], gt[:]), s_ga[s], t)
        return m

    rb, rn, rtok = n_q.finish(dg3, hc_dead, 0)
    cq_tok, old = [None] * 3, [ctx_end, t_free, g_free, nm2.sqf]
    tmp_free = [f_free, f_free]
    for k in range(3):
        cq_tok[k], a = apply_norm(rb, rtok, GQA[:, k:k + 1], k, cqr[:, k, :], ch(cq, k), cq_t, old)
    done(rb, rn, a)
    cqr_dead = a
    rb, rn, rtok = n_k.finish(dg3, n_q.dg_done, 2)
    ck_tok = [None] * 2
    for k in range(2):
        ck_tok[k], a = apply_norm(rb, rtok, GKVA[:, k:k + 1], k, ckr[:, k, 0:T], ch(ck, k, 0, T), ck_t, hc_dead)
    done(rb, rn, a)
    rb, rn, rtok = n_c.finish(dg3, n_k.dg_done, 0)
    for k in range(2):
        tb = tmp[k]
        a = dve.do(lambda e, k=k, tb=tb, r=bank(rb, 0, 256): e.scalar_tensor_tensor(
            tb[:, 0:256], ckr[:, k, T:TA], GKVA[:, k:k + 1], r, ALU.mult, ALU.mult),
            ck_t, rtok, tmp_free[k])
        tmp_free[k] = part(tb[:, 0:256], ck[0][:, k, T:TA], ck[1][:, k, T:TA], a, hc_dead)
        ck_tok[k] = ck_tok[k] + tmp_free[k]
    done(rb, rn, a)
    ckr_dead = a
    ga_free[0] = [n_k.sqf, n_c.sqf]
    ga_free[1] = [nm2.dg_done, t_free]
    ga_free[2], ga_free[3] = list(tmp_free), list(tmp_free)
    for j in range(3):
        ga_block(j)

    Q = at("Q", [8, 768], O_X)
    K_ = at("K", [10, 768], O_V + 28 * KB)
    q_t = [None] * 8
    for i3 in range(3):
        tile = W.take()
        for n2 in range(4):
            b = banks(1)
            for i in range(2):
                n = 2 * n2 + i
                for k in range(3):
                    mm3(psum[:, b, 256 * i:256 * i + 256], ch(cq, k, n * P, n * P + P), wt(tile, k, 256),
                        k == 0, k == 2, (tile[2], cq_tok))
            m = pe.mark()
            dst, src = Q[:, 2 * n2:2 * n2 + 2, 256 * i3:256 * i3 + 256], psum[:, b, :].rearrange("p (a c) -> p a c", a=2)
            if n2 % 2:
                t = act.do(lambda e, d=dst, s=src: e.activation(d, s, ACT.Copy), m, cqr_dead, ckr_dead)
            else:
                t = dve.do(lambda e, d=dst, s=src: e.tensor_copy(d, s), m, cqr_dead, ckr_dead)
            done(b, 1, t)
            q_t[2 * n2] = q_t[2 * n2 + 1] = t
        W.release(tile[3], m)
    cq_dead = m
    k_t = [None] * 10
    tile = W.take()
    for n in range(10):
        b = banks(1)
        for k in range(2):
            mm3(psum[:, b, :], ch(ck, k, n * P, n * P + P), wt(tile, k, 512), k == 0, k == 1, (tile[2], ck_tok))
        m = pe.mark()
        kv = K_[:, n, :].rearrange("p (h d) -> p h d", h=8)
        src = psum[:, b, :].rearrange("p (h d) -> p h d", h=8)
        fr = [cq_dead, ga_free[1], n_c.dg_done]
        if n % 2:
            t = act.do(lambda e, d=kv, s=src: e.activation(d[:, :, 0:64], s, ACT.Copy), m, fr)
        else:
            t = dve.do(lambda e, d=kv, s=src: e.tensor_copy(d[:, :, 0:64], s), m, fr)
        done(b, 1, t)
        t2 = pool.do(lambda e, d=kv, n=n: e.tensor_copy(
            d[:, :, 64:96], kpe[:, n, :].unsqueeze(1).to_broadcast([P, 8, 32])), kpe_tok, fr)
        k_t[n] = [t, t2]
    W.release(tile[3], m)

    sA = [at(f"sA{i}", [768], O_X + (24 + 3 * i) * KB) for i in range(2)]
    rot = at("rot", [256], O_V + 58 * KB)
    ss = small[:, 0:80]
    rr_ = mod[:, 48:64]
    rs8 = at("rs8", [80], O_V + 59 * KB)
    gqs = dve.do(lambda e: e.tensor_scalar(gq[:], gq[:], MLA_SCALE, None, ALU.mult))
    sa_free = [[ga_free[0], t], [ga_free[0], t]]
    rot_free = [None]

    def qk_prep(D, nb, gain, toks, prev):
        rd = []
        for n in range(nb):
            a = act.do(lambda e, n=n: e.activation(sA[n % 2][:], D[:, n, :], ACT.Square), toks[n], sa_free[n % 2])
            t = dve.do(lambda e, n=n: e.tensor_reduce(
                ss[:, 8 * n:8 * n + 8], sA[n % 2][:].rearrange("p (h d) -> p h d", h=8), AX.X, ALU.add), a, prev)
            sa_free[n % 2] = t
        a = act.do(lambda e: e.activation(rs8[:, 0:8 * nb], ss[:, 0:8 * nb], ACT.Sqrt, bias=EPSV, scale=1.0 / 96), t, prev)
        r = dve.do(lambda e: e.reciprocal(rs8[:, 0:8 * nb], rs8[:, 0:8 * nb]), a)
        res = []
        for n in range(nb):
            Dn = D[:, n, :].rearrange("p (h d) -> p h d", h=8)
            t = dve.do(lambda e, Dn=Dn, n=n: e.tensor_tensor(
                Dn, Dn, rs8[:, 8 * n:8 * n + 8].unsqueeze(2).to_broadcast([P, 8, 96]), ALU.mult), r)
            t2 = dve.do(lambda e, Dn=Dn: e.tensor_tensor(
                Dn, Dn, gain[:].unsqueeze(1).to_broadcast([P, 8, 96]), ALU.mult), t, gqs)
            if n >= 8:
                res.append([t2])
                continue
            Dr = Dn[:, :, 64:96].rearrange("p h (a s i) -> p h a s i", a=2, s=2)
            R = rot[:].rearrange("p (h a s i) -> p h a s i", h=8, a=2, s=2)
            tb = rope[:, n, :]
            sn = tb[:, 32:64].rearrange("p (a s i) -> p a s i", a=2, s=2)
            for s in range(2):
                t3 = pool.do(lambda e, s=s, R=R, Dr=Dr, sn=sn: e.tensor_tensor(
                    R[:, :, :, s, :], Dr[:, :, :, 1 - s, :],
                    sn[:, :, s, :].unsqueeze(1).to_broadcast([P, 8, 2, 8]), ALU.mult), t2, rot_free[0])
            t4 = pool.do(lambda e, Dn=Dn, tb=tb: e.tensor_tensor(
                Dn[:, :, 64:96], Dn[:, :, 64:96], tb[:, 0:32].unsqueeze(1).to_broadcast([P, 8, 32]), ALU.mult), t3)
            t5 = pool.do(lambda e, Dn=Dn: e.tensor_tensor(
                Dn[:, :, 64:96], Dn[:, :, 64:96], rot[:].rearrange("p (h d) -> p h d", h=8), ALU.add), t4)
            rot_free[0] = t5
            res.append([t5])
        return res, t2

    rot_free[0] = ga_free[1]
    qn_tok, lastq = qk_prep(Q, 8, gq, q_t, [ga_free[1], sm_free])
    kn_tok, _ = qk_prep(K_, 10, gk, k_t, lastq)
    for j in range(3, 8):
        m = ga_block(j)
    h_dead = m
    V_ = pair("Vv", [10, 768], O_U, O_U + 30 * KB)
    vq = [V_[x][:].rearrange("p n (c a d) -> p n c a d", c=4, a=3) for x in range(2)]
    one_t = [pool.do(lambda e, x=x, n=n: e.memset(f(vq[x][:, n, :, 1, :]), 1.0 - x), h_dead)
             for n in range(10) for x in range(2)]
    tile = W.take()
    vv_tok = [one_t]
    for n in range(10):
        b = banks(1)
        for k in range(2):
            mm3(psum[:, b, :], ch(ck, k, n * P, n * P + P), wt(tile, k, 512), k == 0, k == 1, (tile[2], ck_tok))
        p = part(bank(b).rearrange("p (c a d) -> p c a d", c=4, a=2), vq[0][:, n, :, 0:3:2, :],
                 vq[1][:, n, :, 0:3:2, :], pe.mark(), h_dead)
        done(b, 1, *p)
        vv_tok += p
    ck_dead = pe.mark()
    W.release(tile[3], ck_dead)

    O_HL = O_RING + N_RAW * 4 * KB
    qT = [pair(f"qT{i}", [1024], O_HL + 8 * i * KB, O_HL + (8 * i + 4) * KB) for i in range(2)]
    kT2 = [pair(f"kT2_{i}", [TA], O_V + 10 * i * KB, O_V + (10 * i + 5) * KB) for i in range(2)]
    EX = [at(f"EX{i}", [512], O_HL + (16 + 2 * i) * KB) for i in range(3)]
    EP = [pair("EP0", [512], O_HL + 22 * KB, O_HL + 24 * KB), pair("EP1", [512], O_HL + 26 * KB, O_HL + 28 * KB),
          pair("EP2", [512], O_X + 24 * KB, O_X + 26 * KB)]
    sums = [at(f"sums{i}", [512], O_X + (28 + 2 * i) * KB) for i in range(2)]
    dg4 = at("dg4", [8, P], O_V + 20 * KB)
    old = [h_dead, ck_dead, ga_free, kn_tok]
    for i in range(2):
        for x in range(2):
            kt1 = dve.do(lambda e, i=i, x=x: e.memset(f(kT2[i][x][96:97, :]), 1.0 - x), old)
    qT_free, kT_free = [old, old], [old, old]
    EX_free, EP_free, sum_free = [old] * 3, [old] * 3, [old] * 2
    mxa = small[:, 80:96].rearrange("p (s b) -> p s b", s=2)
    for i in range(8):
        pe.wait(free[i])
    S = psum[:, 0:3, :].rearrange("p b n -> p (b n)")
    S_free, R_free, O_free = [free[0:3]], [free[3], free[4], free[5]], [free[6], free[7]]
    head_tok, max_tok, row_tok = {}, {}, {}
    dg_free = [old]

    def Ocol(c):
        return Q[:, :, 192 * c:192 * c + 128]

    def turn_head(h, who):
        D, nb, dst, fr, toks = ((Q, 8, qT[h % 2], qT_free, qn_tok), (K_, 10, kT2[h % 2], kT_free, kn_tok))[who]
        pe.wait(S_free[0])
        for n in range(nb):
            pe.quiet(lambda e, n=n: e.transpose(
                S[0:96, n * P:n * P + P], D[:, n, 96 * h:96 * h + 96], ident[:]), toks[n])
        q_used[h] = pe.mark()
        p = part(S[0:96, 0:nb * P], dst[0][0:96, 0:nb * P], dst[1][0:96, 0:nb * P], q_used[h], fr[h % 2])
        S_free[0] = p
        head_tok.setdefault(h, []).extend(p)

    def maxima(h, qb):
        pe.wait(S_free[0])
        q = [qT[h % 2][x][0:96, qb * P:qb * P + P] for x in range(2)]
        for c0, c1 in ((0, 512), (512, 1024), (1024, 1280)):
            mm3(S[:, c0:c1], q, [kT2[h % 2][x][0:96, c0:c1] for x in range(2)], True, True, (head_tok[h],))
        t = dve.do(lambda e: e.tensor_reduce(mxa[:, h % 2, qb:qb + 1], S[:, 0:TA], AX.X, ALU.max, negate=True),
                   pe.mark())
        S_free[0] = t
        max_tok[h] = t

    def max_row(h):
        d = dve.do(lambda e: e.tensor_tensor(
            dg4[:], ident[:, None, :].to_broadcast([P, 8, P]),
            mxa[:, h % 2, :].unsqueeze(2).to_broadcast([P, 8, P]), ALU.mult), max_tok[h], dg_free[0])
        pe.wait(S_free[0])
        for i in range(2):
            mm(S[0:97, 512 * i:512 * i + 512], ones[:, 0:97],
               dg4[:, 4 * i:4 * i + 4, :].rearrange("p a b -> p (a b)"), True, True, (d,))
        dg_free[0] = pe.mark()
        p = part(S[96:97, 0:1024], qT[h % 2][0][96:97, :], qT[h % 2][1][96:97, :], dg_free[0], qT_free[h % 2])
        S_free[0] = p
        row_tok[h] = p

    q_used, o_done = {}, {}
    units = [(h, hf, kb) for h in range(8) for hf in range(2) for kb in range(10)]
    ex_tok, ep_tok = {}, {}

    def logits(u):
        h, hf, kb = units[u]
        r = 3 + u % 3
        pe.wait(R_free[u % 3])
        mm3(psum[:, r, :], [kT2[h % 2][x][0:97, kb * P:kb * P + P] for x in range(2)],
            [qT[h % 2][x][0:97, 512 * hf:512 * hf + 512] for x in range(2)], True, True,
            (head_tok[h], row_tok[h], kt1))
        m = pe.mark()
        if (hf, kb) == (1, 9):
            qT_free[h % 2] = kT_free[h % 2] = m
        ex_tok[u] = act.do(lambda e: e.activation(EX[u % 3][:], bank(r), ACT.Exp), m, EX_free[u % 3])
        R_free[u % 3] = ex_tok[u]

    def split(u):
        ep_tok[u] = part(EX[u % 3][:], EP[u % 3][0][:], EP[u % 3][1][:], ex_tok[u], EP_free[u % 3])
        EX_free[u % 3] = ep_tok[u]

    def times_v(u):
        h, hf, kb = units[u]
        o = psum[:, 6 + hf, :]
        if kb == 0:
            pe.wait(O_free[hf])
        c0 = 192 * (h // 2) + 64 * (h % 2)
        mm3(o, [V_[x][:, kb, c0:c0 + 128] for x in range(2)], [EP[u % 3][x][:] for x in range(2)],
            kb == 0, kb == 9, (ep_tok[u], vv_tok))
        EP_free[u % 3] = m = pe.mark()
        if kb == 9:
            r0, s0 = (0, 64) if h % 2 == 0 else (64, 0)
            a = dve.do(lambda e: e.reciprocal(sums[hf][r0:r0 + 64, :], o[s0:s0 + 64, :]), m, sum_free[hf])
            t = dve.do(lambda e: e.tensor_tensor(
                Ocol(h // 2)[r0:r0 + 64, 4 * hf:4 * hf + 4, :],
                o[r0:r0 + 64, :].rearrange("p (b q) -> p b q", b=4),
                sums[hf][r0:r0 + 64, :].rearrange("p (b q) -> p b q", b=4), ALU.mult),
                a, m, q_used[min(7, h + 1)])
            sum_free[hf] = O_free[hf] = t
            o_done[h] = t

    beside = {0: lambda h: turn_head(h, 0), 2: lambda h: turn_head(h, 1), 16: max_row}
    for qb, at_ in enumerate((4, 5, 7, 8, 10, 11, 13, 14)):
        beside[at_] = lambda h, qb=qb: maxima(h, qb)
    for i in sorted(beside):
        beside[i](0)
    n_u = len(units)
    logits(0)
    logits(1)
    split(0)
    for u in range(n_u):
        if u + 2 < n_u:
            logits(u + 2)
        if u + 1 < n_u:
            split(u + 1)
        h, i = u // 20 + 1, u % 20
        if h < 8 and i in beside:
            beside[i](h)
        times_v(u)
    for i in range(3):
        free[i], free[3 + i] = S_free[0], R_free[i]
    free[6], free[7] = O_free
    all_att = [o_done[7], EP_free]
    W.resume(all_att)

    oT = pair("oT", [4, 1024], O_V + 28 * KB, O_V + 44 * KB)
    oT_tok = []
    for c in range(4):
        oT_tok.append(part(Ocol(c), *(y[:, c, :].rearrange("p (b q) -> p b q", b=8) for y in oT),
                           o_done[7], all_att))
    q_dead = oT_tok
    s_x3 = [sem(f"s_xt{i}") for i in range(4)]
    for i in range(4):
        t = pool.dma(lambda e, i=i: e.dma_start(X[:, 2 * i:2 * i + 2, :], A["x1s"][:, 2 * i:2 * i + 2, :]),
                     s_x3[i], q_dead, all_att, spilled)
        x_tok[2 * i] = x_tok[2 * i + 1] = t
    gal = [at(f"gal{i}", [1024], O_V + 4 * i * KB) for i in range(2)]
    tsl = [at(f"tsl{i}", [1024], O_V + (8 + 4 * i) * KB) for i in range(2)]
    mtm = [at(f"mtm{i}", [1024], O_V + (16 + 4 * i) * KB) for i in range(2)]
    s_gl = [sem(f"s_gl{i}") for i in range(2)]
    s_tl = [sem(f"s_tl{i}") for i in range(2)]
    gl_free, tl_free, mt_free = [all_att] * 2, [all_att] * 2, [all_att] * 2
    gl_tok, tl_tok = {}, {}

    def gates(j):
        i = j % 2
        gl_tok[j] = pool.dma(lambda e: e.dma_start(gal[i][:], A["gas"][j]), s_gl[i], gl_free[i], ga_free)
        tl_tok[j] = pool.dma(lambda e: e.dma_start(tsl[i][:], A["ts"][j]), s_tl[i], tl_free[i], t_free)

    M = pair("M", [8, 1024], O_U, O_U + 32 * KB)
    m_tok = [None] * 8
    gates(0)
    gates(1)
    for j in range(8):
        if j % 2 == 0:
            ao_tile = W.take()
        z = j % 2
        ts = []
        for i, (b, m) in enumerate(proj_T(oT, oT_tok, nk=4, n_w=256, sub=128 * (j % 2), tile=ao_tile)):
            sl = slice(512 * i, 512 * i + 512)
            t = dve.do(lambda e, b=b, sl=sl, z=z: e.tensor_tensor(mtm[z][:, sl], bank(b), gal[z][:, sl], ALU.mult),
                       m, gl_tok[j], mt_free[z])
            done(b, 1, t)
            ts.append(t)
        if j % 2 == 1:
            W.release(ao_tile[3], m)
        gl_free[z] = t
        t = dve.do(lambda e, z=z: e.tensor_tensor(mtm[z][:], mtm[z][:], tsl[z][:], ALU.add), ts, tl_tok[j])
        tl_free[z] = t
        if j < 6:
            gates(j + 2)
        m_tok[j] = part(mtm[z][:], M[0][:, j, :], M[1][:, j, :], t, all_att)
        mt_free[z] = m_tok[j]
    oT_dead = m
    nm = Norm(INV1024, T, sq, oT_dead)
    for n in range(8):
        ts = []
        for i, (b, m) in enumerate(proj_T(M, m_tok)):
            sl = slice(512 * i, 512 * i + 512)
            t = dve.do(lambda e, b=b, sl=sl, n=n: e.scalar_tensor_tensor(
                X[:, n, sl], bank(b), GT1[:, n:n + 1], X[:, n, sl], ALU.mult, ALU.add), m, x_tok[n])
            done(b, 1, t)
            ts.append(t)
        x_tok[n] = ts
        nm.add(X[:, n, :], ts, last=n == 7)
    m_dead = m
    H2 = at("H2", [8, 1024], O_U)
    wr = at("wr", [8, 16], O_CONST + 6144)
    s_wr = sem("s_wr")
    wr_tok = pool.dma(lambda e: e.dma_start(wr[:], A["w_r"]), s_wr)
    tm2 = [at(f"tm2_{i}", [1024], O_V + (16 + 4 * i) * KB) for i in range(2)]
    t2_free = list(mt_free)
    rb, rn, rtok = nm.finish(dg, oT_dead, 0)
    lb = banks(1)
    held.add(lb)
    h2_tok = [None] * 8
    for k in range(8):
        tb = tm2[k % 2]
        a = dve.do(lambda e, k=k, tb=tb, r=two(rb): e.scalar_tensor_tensor(
            tb[:], X[:, k, :], SC2[:, k:k + 1], r, ALU.mult, ALU.mult), rtok, x_tok[k], t2_free[k % 2])
        h2_tok[k] = act.do(lambda e, k=k, tb=tb: e.activation(
            H2[:, k, :], tb[:], ACT.Identity, bias=SH2[:, k:k + 1]), a, m_dead)
        t2_free[k % 2] = h2_tok[k]
        for n in range(8):
            mm(psum[:, lb, 16 * n:16 * n + 16], H2[:, k, n * P:n * P + P], wr[:, k, :],
               k == 0 and n == 0, k == 7 and n == 7, (h2_tok[k], wr_tok), True)
    done(rb, rn, a)
    log_m = pe.mark()
    aff = at("aff", [8, 16], O_U + 44 * KB)
    lg = psum[:, lb, 0:128].rearrange("p (n e) -> p n e", n=8)
    sm8, su8 = small[:, 0:8], small[:, 8:16]
    bc = lambda v: v.unsqueeze(2).to_broadcast([P, 8, 16])
    t = dve.do(lambda e: e.tensor_reduce(sm8, lg, AX.X, ALU.max), log_m, o_done[7])
    t = dve.do(lambda e: e.tensor_tensor(aff[:], lg, bc(sm8), ALU.subtract), t, m_dead)
    done(lb, 1, t)
    held.discard(lb)
    t = act.do(lambda e: e.activation(aff[:], aff[:], ACT.Exp), t)
    t = dve.do(lambda e: e.tensor_reduce(su8, aff[:], AX.X, ALU.add), t)
    t = dve.do(lambda e: e.reciprocal(su8, su8), t)
    aff_t = dve.do(lambda e: e.tensor_tensor(aff[:], aff[:], bc(su8), ALU.mult), t)
    b = banks(2)
    for n in range(8):
        pe.quiet(lambda e, n=n, b=b: e.transpose(
            two(b)[0:16, n * P:n * P + P], aff[:, n, :], ident[:]), aff_t)
    m = pe.mark()
    cur = [at(f"cur{i}", [1024], O_U + (45 + 4 * i) * KB) for i in range(2)]
    vals = at("vals", [128], O_U + 53 * KB)
    idx = at("idx", [128], O_U + 54 * KB, U32)
    idxf = at("idxf", [128], O_U + 55 * KB)
    gcol = at("gcol", [16], O_U + 56 * KB)
    icol = at("icol", [16], O_U + 57 * KB, U32)
    c_t = dve.do(lambda e, b=b: e.tensor_copy(cur[0][0:16, :], two(b)[0:16, :]), m, m_dead)
    done(b, 2, c_t)
    row = [at(f"row{i}", [1024], O_V + (40 + 4 * i) * KB) for i in range(5)]
    s_row = [sem(f"s_row{i}") for i in range(5)]
    row_free = [[oT_dead, nm.m, nm.dg_done, m_dead]] * 5
    nrow = [0]

    def rows(srcs, toks, dram, n):
        i = nrow[0] % 5
        nrow[0] += 1
        b = banks(2)
        for k in range(8):
            pe.quiet(lambda e, k=k, b=b: e.transpose(
                two(b)[:, k * P:k * P + P], srcs[:, k, n * P:n * P + P], ident[:]), toks)
        m = pe.mark()
        t = act.do(lambda e: e.activation(row[i][:], two(b), ACT.Copy), m, row_free[i])
        done(b, 2, t)
        row_free[i] = pool.dma(lambda e: e.dma_start(dram[n * P:n * P + P, :], row[i][:]), s_row[i], t)
        return m

    for n in range(8):
        rows(H2, h2_tok, A["h2s"], n)
    h2_saved = list(row_free)
    for n in range(8):
        x2_m = rows(X, x_tok, out, n)
    rows_saved = list(row_free)

    for r in range(16):
        c0, c1 = cur[r % 2][0:16, :], cur[1 - r % 2][0:16, :]
        v8, i8 = vals[0:16, 8 * r:8 * r + 8], idx[0:16, 8 * r:8 * r + 8]
        t = dve.do(lambda e, v8=v8, c0=c0: e.max(v8, c0), c_t)
        t2 = dve.do(lambda e, v8=v8, c0=c0, i8=i8: e.max_index(i8, v8, c0), t)
        if r < 15:
            c_t = dve.do(lambda e, v8=v8, c0=c0, c1=c1: e.match_replace(c1, v8, c0, -1.0), t2)
    t = dve.do(lambda e: e.tensor_copy(idxf[0:16, :], idx[0:16, :]), t2)
    b = banks(1)
    pe.quiet(lambda e, b=b: e.transpose(psum[:, b, 0:16], vals[0:16, :], ident[0:16, 0:16]), t)
    pe.quiet(lambda e, b=b: e.transpose(psum[:, b, 16:32], idxf[0:16, :], ident[0:16, 0:16]), t)
    m = pe.mark()
    g_t = dve.do(lambda e, b=b: e.tensor_copy(gcol[:], psum[:, b, 0:16]), m)
    i_t = dve.do(lambda e, b=b: e.tensor_copy(icol[:], psum[:, b, 16:32]), m)
    done(b, 1, g_t, i_t)
    grown = [at(f"rawe{i}", [1024], O_V + 4 * i * KB) for i in range(15)]
    s_grown = [sem(f"s_rawe{i}") for i in range(15)]
    gfree = [[m_dead, t2_free, oT_dead, gl_free, tl_free, mt_free] + ([rows_saved] if i >= 10 else []) for i in range(15)]
    gx = [at(f"rawx{i}", [1024], O_X + 4 * i * KB) for i in range(8)]
    s_gx = [sem(f"s_rawx{i}") for i in range(8)]
    W.grow(grown + gx, s_grown + s_gx, gfree + [[x2_m]] * 8)
    W.pool_lo = False

    dg2 = at("dg2", [8, P], O_U + 60 * KB)
    g2b = at("g2b", [1024], O_U + 40 * KB)
    d = dve.do(lambda e: e.tensor_tensor(
        dg2[:], ident[:, None, :].to_broadcast([P, 8, P]), GT2.unsqueeze(2).to_broadcast([P, 8, P]), ALU.mult),
        mod_tok, m_dead)
    b = banks(2)
    for i in range(2):
        mm(psum[:, b + i, :], ones[:], dg2[:, 4 * i:4 * i + 4, :].rearrange("p a b -> p (a b)"), True, True, (d,))
    g2_t = act.do(lambda e, b=b: e.activation(g2b[:], two(b), ACT.Copy), pe.mark(), m_dead)
    done(b, 2, g2_t)

    xg = [at(f"xg{i}", [1024], O_U + 4 * i * KB) for i in range(2)]
    xe = [pair(f"xe{i}", [8, P], O_U + (8 + 8 * i) * KB, O_U + (12 + 8 * i) * KB) for i in range(2)]
    hs = at("hs", [512], O_U + 24 * KB)
    hv = at("hv", [512], O_U + 26 * KB)
    hT = pair("hT", [4, P], O_U + 28 * KB, O_U + 30 * KB)
    ye = [at(f"ye{i}", [1024], O_U + (32 + 4 * i) * KB) for i in range(2)]
    s_xg = [sem(f"s_xg{i}") for i in range(2)]
    s_ye = [sem(f"s_ye{i}") for i in range(2)]
    h2_dead = x2_m
    xg_free, xe_free, ye_free = [h2_dead] * 2, [h2_dead] * 2, [h2_dead] * 2
    xg_tok, xe_tok = {}, {}

    def gather(e_):
        i = e_ % 2
        xg_tok[e_] = pool.dma(lambda e: e.indirect_dma_start(
            out=xg[i][:], out_offset=None, in_=A["h2s"],
            in_offset=bass.IndirectOffsetOnAxis(ap=icol[:, e_:e_ + 1], axis=0)), s_xg[i], xg_free[i], h2_saved, i_t)

    def turn_rows(e_):
        i = e_ % 2
        b = banks(2)
        for k in range(8):
            pe.quiet(lambda e, k=k, b=b: e.transpose(
                two(b)[:, k * P:k * P + P], xg[i][:, k * P:k * P + P], ident[:]), xg_tok[e_])
        m = pe.mark()
        xg_free[i] = m
        x0, x1 = (y[:].rearrange("p a b -> p (a b)") for y in xe[i])
        xe_tok[e_] = part(two(b), x0, x1, m, xe_free[i])
        done(b, 2, *xe_tok[e_])

    gather(0)
    gather(1)
    turn_rows(0)
    hs_free, hv_free, hT_free = h2_dead, h2_dead, h2_dead
    scat = rows_saved
    for e_ in range(16):
        i = e_ % 2
        ba, bb = banks(1), banks(1)
        for c in range(4):
            for bq in (ba, bb):
                tile = W.take()
                for k2 in range(2):
                    k = 2 * c + k2
                    mm3(psum[:, bq, :], (xe[i][0][:, k, :], xe[i][1][:, k, :]), wt(tile, k2, 512),
                        k == 0, k == 7, (tile[2], xe_tok[e_]))
                m = pe.mark()
                W.release(tile[3], m)
                if bq == ba:
                    ma = m
        xe_free[i] = m
        if e_ < 14:
            gather(e_ + 2)
        t = act.do(lambda e, ba=ba: e.activation(hs[:], bank(ba), ACT.Silu), ma, hs_free)
        done(ba, 1, t)
        t = dve.do(lambda e, bb=bb: e.tensor_tensor(hv[:], bank(bb), hs[:], ALU.mult), t, m, hv_free)
        done(bb, 1, t)
        hs_free = t
        if e_ < 15:
            turn_rows(e_ + 1)
        b = banks(1)
        for c in range(4):
            pe.quiet(lambda e, c=c, b=b: e.transpose(psum[:, b, c * P:c * P + P], hv[:, c * P:c * P + P], ident[:]), t)
        m = pe.mark()
        hv_free = m
        y0, y1 = (y[:].rearrange("p a b -> p (a b)") for y in hT)
        hT_t = part(bank(b), y0, y1, m, hT_free)
        done(b, 1, *hT_t)
        b = banks(2)
        for c in range(4):
            tile = W.take()
            for j in range(2):
                mm3(psum[:, b + j, :], (hT[0][:, c, :], hT[1][:, c, :]),
                    (tile[0][:, 512 * j:512 * j + 512], tile[1][:, 512 * j:512 * j + 512]), c == 0, c == 3,
                    (tile[2], hT_t))
            m = pe.mark()
            W.release(tile[3], m)
        hT_free = m
        t = dve.do(lambda e, b=b, i=i, e_=e_: e.scalar_tensor_tensor(
            ye[i][:], two(b), gcol[:, e_:e_ + 1], g2b[:], ALU.mult, ALU.mult), m, g2_t, g_t, ye_free[i])
        done(b, 2, t)
        scat = pool.dma(lambda e, i=i, e_=e_: e.indirect_dma_start(
            out=out, out_offset=bass.IndirectOffsetOnAxis(ap=icol[:, e_:e_ + 1], axis=0),
            in_=ye[i][:], in_offset=None, compute_op=ALU.add), s_ye[i], t, scat)
        ye_free[i] = scat
    finish_program([scat])


def slopes():
    return np.exp2(-8.0 * np.arange(1, 17, dtype=np.float32) / 16).astype(np.float32)


def constants():
    c = {"ident": np.eye(128, dtype=np.float32), "ones": np.ones((128, 128), np.float32)}
    qi, kj = np.arange(128)[:, None], np.arange(256)[None, :]
    dist = (128 + qi - kj).astype(np.float32)
    ok = (dist >= 0) & (dist < 128)
    sl = slopes()
    b = np.stack([np.where(ok, -sl[h] * dist, np.float32(-1e30)) for h in range(16)]).astype(np.float32)
    c["bias"] = np.ascontiguousarray(np.stack([b[:8], b[8:]], 1).transpose(0, 2, 1, 3))
    inv = (1.0 / (np.float32(10000.0) ** (np.arange(8, dtype=np.float32) / np.float32(8)))).astype(np.float32)
    t = np.arange(1024)

    def tab(pos):
        a = pos.astype(np.float32)[:, None] * inv[None]
        return np.concatenate([a, a], -1)

    ang = np.concatenate([tab(t // 64), tab(t % 64)], -1)
    sgn = np.tile(np.concatenate([-np.ones(8), np.ones(8)]), 2).astype(np.float32)
    r = np.concatenate([np.cos(ang), np.sin(ang) * sgn], -1).astype(np.float32)
    c["rope"] = np.ascontiguousarray(r.reshape(8, 128, 64).transpose(1, 0, 2))
    n = np.arange(128)
    a = 2 * np.pi * (np.outer(n, n) % 128) / 128
    s = 1.0 / np.sqrt(1024.0 * 128.0)
    c["dft_c"] = np.concatenate([np.cos(a) * s, np.sin(a) * s], -1).astype(np.float32)
    n = np.arange(1024)
    a = 2 * np.pi * (np.outer(n, n) % 1024) / 1024
    c["dft_t"] = np.concatenate([np.cos(a), -np.sin(a)]).astype(np.float32).reshape(16, 128, 1024)
    return c


def lay_out(x, attn_norm, mlp_norm, final_norm, swa_w_qkv, swa_sinks, swa_w_o, mlp_w_up, mlp_w_down,
            c_2, ctx_2, c_ctx_2, w_mod_2, b_mod_2, norm1_g_2, w_in_2, q_a_norm_g_2, kv_a_norm_g_2,
            w_q_up_2, w_kv_up_2, q_norm_g_2, k_norm_g_2, w_o_attn_2, w_fourier_2, w_out_2, norm2_g_2,
            w_router_2, w_e_gate_2, w_e_up_2, w_e_down_2, **unused):
    c = constants()

    def cols(w, n):
        k, m = w.shape
        return np.ascontiguousarray(
            w.reshape(k // 128, 128, m // n, n).transpose(2, 1, 0, 3).reshape(m // n, 128, k // 128 * n))

    def vec(v):
        return v.reshape(-1, 128).T

    r = dict(c)
    r["xT"] = np.ascontiguousarray(x[0].T.reshape(8, 128, 1024).transpose(1, 0, 2))
    r["ctxT"] = np.ascontiguousarray(ctx_2[0].T.reshape(8, 128, 256).transpose(1, 0, 2))
    v = np.zeros((128, 128), np.float32)
    for a, o in ((attn_norm[0], 0), (mlp_norm[0], 8), (final_norm, 16), (norm1_g_2[0], 24), (norm2_g_2[0], 32),
                 (q_a_norm_g_2[0], 40), (kv_a_norm_g_2[0], 43), (b_mod_2[0], 48)):
        v[:, o:o + a.size // 128] = vec(a)
    pairs = np.arange(16).reshape(2, 8).T.reshape(-1)
    v[:, 96:112] = swa_sinks[0][pairs][None, :]
    v[:, 112:117] = np.array([EPS, 1 / 1024, 1 / 384, 1 / 256, 1 / 96], np.float32)
    r["vec"] = v
    r["gq"] = np.ascontiguousarray(np.broadcast_to(q_norm_g_2[0], (128, 96)))
    r["gk"] = np.ascontiguousarray(np.broadcast_to(k_norm_g_2[0], (128, 96)))
    w = swa_w_qkv[0]
    r["w_k"], r["w_v"] = cols(w[:, 1024:1152], 128), cols(w[:, 1152:1280], 128)
    r["w_q"] = cols(w[:, 0:1024].reshape(1024, 16, 64)[:, pairs].reshape(1024, 1024), 128)
    r["w_so"] = cols(swa_w_o[0].reshape(16, 64, 1024)[pairs].reshape(1024, 1024), 128)
    r["w_up"] = cols(mlp_w_up[0], 128)
    r["w_dn"] = np.ascontiguousarray(
        mlp_w_down[0].reshape(8, 4, 128, 4, 256).transpose(0, 3, 2, 1, 4).reshape(32, 128, 1024))
    r["w_mod"] = np.ascontiguousarray(w_mod_2[0].T.reshape(48, 128, 2, 512).transpose(0, 2, 1, 3).reshape(96, 128, 512))
    r["c_b"] = np.ascontiguousarray(np.broadcast_to(c_2[0], (128, 1024)))
    r["cc_b"] = np.ascontiguousarray(np.broadcast_to(c_ctx_2, (128, 1024)))
    w = w_in_2[0]
    r["w_qa"], r["w_kva"] = cols(w[:, 0:384], 128), cols(w[:, 384:640], 128)
    r["w_kpe"] = cols(w[:, 640:672], 32)
    r["w_f"] = cols(w[:, 672:1184], 128)
    r["w_ga"], r["w_gb"] = cols(w[:, 1184:2208], 128), cols(w[:, 2208:3232], 128)
    r["w_qup"] = cols(w_q_up_2[0], 256)
    w = w_kv_up_2[0].reshape(256, 8, 128)
    r["w_kup"] = cols(w[:, :, :64].reshape(256, 512), 512)
    r["w_vup"] = cols(w[:, :, 64:].reshape(256, 512), 512)
    r["w_ao"], r["w_fo"] = cols(w_o_attn_2[0], 256), cols(w_fourier_2[0], 256)
    r["w_out"] = cols(w_out_2[0], 128)
    r["w_r"] = np.ascontiguousarray(w_router_2[0].reshape(8, 128, 16).transpose(1, 0, 2))
    g = w_e_gate_2[0].reshape(16, 4, 2, 128, 512).transpose(0, 1, 3, 2, 4).reshape(16, 4, 128, 1024)
    u = w_e_up_2[0].reshape(16, 4, 2, 128, 512).transpose(0, 1, 3, 2, 4).reshape(16, 4, 128, 1024)
    d = w_e_down_2[0].reshape(16, 4, 128, 1024)
    r["w_e"] = np.stack([g[:, 0], u[:, 0], g[:, 1], u[:, 1], g[:, 2], u[:, 2], g[:, 3], u[:, 3],
                         d[:, 0], d[:, 1], d[:, 2], d[:, 3]], 1).reshape(192, 128, 1024)
    return r


SCRATCH = {"x1s": (128, 8, 1024), "ts": (8, 128, 1024), "gas": (8, 128, 1024), "h2s": (1024, 1024)}


def kernel(**inputs):
    import concourse.bacc as _bacc
    from concourse.bass_utils import run_bass_kernel_spmd as _run

    nc = _bacc.Bacc("TRN2", target_bir_lowering=False, num_devices=1)
    arrays, A = {}, {}
    for name, a in lay_out(**{k: np.asarray(v) for k, v in inputs.items()}).items():
        arrays[f"in_{name}"] = a
        A[name] = nc.dram_tensor(f"in_{name}", a.shape, F32, kind="ExternalInput").ap()
    for name, shape in SCRATCH.items():
        A[name] = nc.dram_tensor(name, shape, F32, kind="Internal").ap()
    out = nc.dram_tensor("out_0", (1024, 1024), F32, kind="ExternalOutput").ap()
    build(nc, A, out)
    r = _run(nc, [arrays], core_ids=[0])
    return r.results[0]["out_0"].reshape(1, 1024, 1024)
```

```python
from contextlib import ExitStack

import numpy as np

import concourse.bass as bass
from concourse import mybir

F32 = mybir.dt.float32
F32R = mybir.dt.float32r
U32 = mybir.dt.uint32
ALU = mybir.AluOpType
ACT = mybir.ActivationFunctionType
AX = mybir.AxisListType

P = 128
T = 1024
TC = 256
TA = T + TC
EPS = 1e-6
KB = 1024
MLA_SCALE = 96.0 ** -0.5

O_CONST = 0
O_RING = 7 * KB
N_RAW, N_HL = 3, 4
O_X = O_RING + N_RAW * 4 * KB + N_HL * 8 * KB
O_U = O_X + 32 * KB
O_V = O_U + 64 * KB
ARENA = O_V + 60 * KB


class Sem:

    def __init__(self, handle):
        self.handle, self.n = handle, 0


class Queue:

    def __init__(self, sem):
        self.ops, self.sem, self.waited = [], sem, {}

    def wait(self, *tokens):
        for t in tokens:
            if t is None:
                continue
            if isinstance(t, list):
                self.wait(*t)
                continue
            sem, value = t
            if self.waited.get(id(sem), 0) < value:
                self.waited[id(sem)] = value
                self.ops.append(("wait", sem, value))

    def do(self, fn, *tokens):
        self.wait(*tokens)
        self.sem.n += 1
        self.ops.append(("do", fn, self.sem, 1))
        return (self.sem, self.sem.n)

    def quiet(self, fn, *tokens):
        self.wait(*tokens)
        self.ops.append(("do", fn, None, 0))

    def mark(self):
        _, fn, sem, _ = self.ops[-1]
        if sem is not None:
            return (self.sem, self.sem.n)
        self.sem.n += 1
        self.ops[-1] = ("do", fn, self.sem, 1)
        return (self.sem, self.sem.n)

    def dma(self, fn, sem, *tokens):
        self.wait(*tokens)
        sem.n += 16
        self.ops.append(("do", fn, sem, 16))
        return (sem, sem.n)

    def emit(self, eng):
        for op in self.ops:
            if op[0] == "wait":
                eng.wait_ge(op[1].handle, op[2])
            else:
                ins = op[1](eng)
                if op[2] is not None:
                    ins.then_inc(op[2].handle, op[3])


def build(nc, A, out):
    ctx = ExitStack()
    with ctx:
        _program(nc, A, out, ctx)


def _program(nc, A, out, ctx):
    def sem(name):
        return Sem(ctx.enter_context(nc.semaphore(name)))

    pe, act, dve, pool, sp = (Queue(sem("s_" + n)) for n in ("pe", "act", "dve", "pool", "sp"))
    base = (nc.sbuf_base + 31) // 32 * 32
    ctx.enter_context(nc.sbuf_tensor("arena", [P, ARENA // 4], F32))
    psum = ctx.enter_context(nc.psum_tensor("psum", [P, 8, 512], F32))

    def at(name, shape, off, dt=F32):
        return nc.alloc_sbuf_tensor_at(name, [P] + list(shape), dt, offset=base + off)

    def pair(name, shape, off_hi, off_lo):
        return at(name + "_hi", shape, off_hi, F32R), at(name + "_lo", shape, off_lo, F32R)

    def f(ap):
        return ap.bitcast(F32)

    ident = at("ident", [128], O_CONST)
    ones = at("ones", [128], O_CONST + 512)
    vec = at("vec", [128], O_CONST + 1024)
    mod = at("mod", [64], O_CONST + 1536)
    gq = at("gq", [96], O_CONST + 2048)
    gk = at("gk", [96], O_CONST + 2048 + 384)
    rope = at("rope", [8, 64], O_CONST + 3072)
    small = at("small", [128], O_CONST + 5120)
    st = at("st", [4, 16], O_CONST + 5632)
    modb = at("modb", [64], O_CONST + 5888)
    G1, G2, GF = vec[:, 0:8], vec[:, 8:16], vec[:, 16:24]
    N1, N2 = vec[:, 24:32], vec[:, 32:40]
    GQA, GKVA = vec[:, 40:43], vec[:, 43:45]
    BMOD = vec[:, 48:96]
    SINK = vec[:, 96:112]
    EPSV = vec[:, 112:113]
    INV1024, INV384, INV256 = vec[:, 113:114], vec[:, 114:115], vec[:, 115:116]

    s_c = sem("s_const")
    c_tok = None
    for dst, src in ((ident, "ident"), (ones, "ones"), (vec, "vec"), (gq, "gq"), (gk, "gk"), (rope, "rope")):
        c_tok = pool.dma(lambda e, d=dst, s=src: e.dma_start(d[:], A[s]), s_c)
    for q in (pe, act, dve):
        q.wait(c_tok)

    raws = [(O_RING + i * 4 * KB) for i in range(N_RAW)]
    raw_t = [at(f"raw{i}", [1024], o) for i, o in enumerate(raws)]
    raw_s = [sem(f"s_raw{i}") for i in range(N_RAW)]
    hl = [pair(f"w{i}", [1024], O_RING + N_RAW * 4 * KB + i * 8 * KB, O_RING + N_RAW * 4 * KB + i * 8 * KB + 4 * KB)
          for i in range(N_HL)]

    class Stream:
        def __init__(self, raw, sems):
            self.raw, self.sems = raw, sems
            self.slot_free = [None] * len(raw)
            self.spec, self.loaded, self.parted, self.used = [], 0, 0, 0
            self.where, self.tok = {}, {}
            self.next_slot = 0
            self.ready, self.place = {}, {}
            self.idle = [(0, None), (1, None)]
            self.pool_lo = False
            self.limit = 1 << 30

        def load(self):
            t = self.loaded
            name, i, width = self.spec[t]
            slot = self.next_slot % len(self.raw)
            self.next_slot += 1
            dst = self.raw[slot]
            self.where[t] = slot
            sp.wait(self.slot_free[slot])
            self.tok[t] = sp.dma(lambda e: e.dma_start(dst[:, 0:width], A[name][i]), self.sems[slot])
            self.loaded += 1

        def grow(self, raw, sems, free):
            keep = {self.where[t]: t for t in range(self.parted, self.loaded)}
            order = sorted(keep, key=lambda s: keep[s])
            idle = [s for s in range(len(self.raw)) if s not in keep]
            names = order + idle
            self.raw, old = [self.raw[s] for s in names] + raw, self.raw
            self.sems = [self.sems[s] for s in names] + sems
            self.slot_free = [self.slot_free[s] for s in names] + free
            for pos, s in enumerate(order):
                self.where[keep[s]] = pos
            self.next_slot = len(order)

        def part(self):
            t = self.parted
            width = self.spec[t][2]
            place, free = self.idle.pop(0)
            self.place[t] = place
            slot, (hi, lo) = self.where[t], hl[place]
            raw = self.raw[slot]
            h = act.do(lambda e: e.activation(hi[:, 0:width], raw[:, 0:width], ACT.Copy), self.tok[t], free)
            q = pool if self.pool_lo and t % 3 == 0 else dve
            l = q.do(lambda e: e.tensor_tensor(lo[:, 0:width], raw[:, 0:width], f(hi[:, 0:width]), ALU.subtract),
                     h, self.tok[t], free)
            self.ready[t] = [h, l]
            self.slot_free[slot] = [h, l]
            self.parted += 1

        def fill(self):
            while self.loaded < len(self.spec) and self.loaded < self.parted + len(self.raw):
                self.load()

        def take(self, ahead=None):
            t = self.used
            self.used += 1
            upto = t + (N_HL - 1 if ahead is None else ahead)
            self.fill()
            while self.parted < min(len(self.spec), self.limit) and self.parted <= upto and self.idle:
                self.part()
                self.fill()
            assert self.parted > t
            hi, lo = hl[self.place[t]]
            return hi, lo, self.ready[t], t

        def prepare(self, n):
            self.fill()
            while self.parted < min(self.used + n, self.limit) and self.idle:
                self.part()
                self.fill()

        def release(self, t, token):
            self.idle.append((self.place[t], token))

        def lend(self, places, token):
            self.idle += [(p, token) for p in places]

        def resume(self, *tokens):
            self.limit = 1 << 30
            self.idle = [(p, list(tokens)) for p in range(N_HL)]

    W = Stream(raw_t, raw_s)

    def plan(name, n, width=1024):
        for i in range(n):
            W.spec.append((name, i, width))

    plan("w_k", 1)
    plan("w_v", 1)
    plan("w_q", 8)
    plan("w_so", 8)
    W.spec += [("w_up", i, 1024) for i in range(6)]
    for g in range(8):
        W.spec += [("w_dn", 4 * g + i, 1024) for i in range(4)]
        W.spec += [("w_up", i, 1024) for i in range(4 * g + 6, min(4 * g + 10, 32))]
    plan("w_f", 4)
    plan("dft_t", 16)
    for j in range(8):
        W.spec.append(("w_gb", j, 1024))
        if j % 2 == 0:
            W.spec.append(("w_fo", j // 2, 1024))
    plan("w_qa", 3)
    plan("w_kva", 2)
    plan("w_kpe", 1, 256)
    W.spec += [("w_ga", j, 1024) for j in range(3)]
    plan("w_qup", 3, 768)
    plan("w_kup", 1)
    W.spec += [("w_ga", j, 1024) for j in range(3, 8)]
    plan("w_vup", 1)
    W.limit = len(W.spec)
    plan("w_ao", 4)
    plan("w_out", 8)
    plan("w_e", 192)

    free = [None] * 8
    turn = [0]
    held = set()

    def banks(n=1):
        b = turn[0]
        while b + n > 8 or held & set(range(b, b + n)):
            b = (b + 1) % 8
        turn[0] = (b + n) % 8
        for i in range(b, b + n):
            pe.wait(free[i])
            free[i] = None
        return b

    def done(b, n, *tokens):
        for i in range(b, b + n):
            free[i] = list(tokens)

    def bank(b, lo=0, hi=512, n=1):
        return psum[:, b, lo:hi] if n == 1 else psum[:, b:b + n, :].rearrange("p b n -> p (b n)")[:, lo:hi]

    def mm(o, l, r, start, stop, tokens=(), skip=False):
        pe.quiet(lambda e: e.matmul(o, l, r, start=start, stop=stop, skip_group_check=skip), *tokens)

    def mm3(o, l, r, first, last, tokens=()):
        mm(o, l[0], r[0], first, False, tokens)
        mm(o, l[0], r[1], False, False)
        mm(o, l[1], r[0], False, last)

    def part(src, hi, lo, tokens, free_tok=None, bias=None, q=None):
        if bias is None:
            h = act.do(lambda e: e.activation(hi, src, ACT.Copy), tokens, free_tok)
            l = (q or dve).do(lambda e: e.tensor_tensor(lo, src, f(hi), ALU.subtract), tokens, h, free_tok)
        else:
            h = act.do(lambda e: e.activation(hi, src, ACT.Identity, bias=bias), tokens, free_tok)
            l = dve.do(lambda e: e.scalar_tensor_tensor(lo, src, bias, f(hi), ALU.add, ALU.subtract),
                       tokens, h, free_tok)
        return [h, l]

    class Norm:

        def __init__(self, inv, width, sq, tokens_sq=None):
            self.inv, self.w, self.nb = inv, width, width // P
            self.sq, self.sqf, self.k = sq, [tokens_sq] * len(sq), 0
            self.acc = len(sq) > 1
            if not self.acc:
                self.b = banks(1)
                held.add(self.b)

        def sum(self, src, first, last, t):
            for tb in range(self.nb):
                mm(psum[:, self.b, tb:tb + 1], src[:, tb * P:(tb + 1) * P], self.inv,
                   first and tb == 0, last and tb == self.nb - 1, (t,), True)
            self.m = pe.mark()

        def add(self, x, *tokens, last=False, scale=1.0):
            i = 1 + self.k % (len(self.sq) - 1) if self.acc and self.k > 0 else 0
            sq = self.sq[i]
            t = act.do(lambda e: e.activation(sq[:, 0:self.w], x, ACT.Square, scale=scale), *tokens, self.sqf[i])
            if self.acc:
                if self.k > 0:
                    s0 = self.sq[0]
                    t = dve.do(lambda e: e.tensor_tensor(s0[:, 0:self.w], s0[:, 0:self.w], sq[:, 0:self.w], ALU.add),
                               t, self.total)
                    self.sqf[i] = t
                self.total = t
            else:
                self.sum(sq, self.k == 0, last, t)
                self.sqf[0] = self.m
            self.k += 1

        def finish(self, dg, dg_free, s):
            if self.acc:
                self.b = banks(1)
                self.sum(self.sq[0], True, True, self.total)
                self.sqf[0] = self.m
            nb = self.nb
            sd, r = st[:, s, 0:nb], st[:, s + 1, 0:nb]
            a = act.do(lambda e: e.activation(sd, psum[:, self.b, 0:nb], ACT.Sqrt, bias=EPSV), self.m, rs_free[0])
            done(self.b, 1, a)
            held.discard(self.b)
            v = dve.do(lambda e: e.reciprocal(r, sd), a, rs_free[0])
            d = dve.do(lambda e: e.tensor_tensor(
                dg[:, 0:nb, :], ident[:, None, :].to_broadcast([P, nb, P]),
                r.unsqueeze(2).to_broadcast([P, nb, P]), ALU.mult), v, dg_free)
            n = (nb + 3) // 4
            b = banks(n)
            for i in range(n):
                w = min(4, nb - 4 * i)
                mm(psum[:, b + i, 0:w * P], ones[:], dg[:, 4 * i:4 * i + w, :].rearrange("p a b -> p (a b)"),
                   True, True, (d,))
            rs_free[0] = [d]
            self.dg_done = pe.mark()
            return b, n, self.dg_done

    rs_free = [None]

    def two(b, c0=0, c1=1024):
        return psum[:, b:b + 2, :].rearrange("p b n -> p (b n)")[:, c0:c1]

    def finish_program(last_tokens):
        sp.wait(*last_tokens, *[(x, x.n) for x in W.sems])
        with nc.Block() as block:
            @block.sync
            def _(e):
                sp.emit(e)

            @block.gpsimd
            def _(e):
                pool.emit(e)

            @block.scalar
            def _(e):
                act.emit(e)

            @block.vector
            def _(e):
                dve.emit(e)

            @block.tensor
            def _(e):
                pe.emit(e)


    X = at("X", [8, 1024], O_X)
    s_x = [sem(f"s_x{i}") for i in range(4)]
    x_tok = [None] * 8
    for i in range(4):
        t = sp.dma(lambda e, i=i: e.dma_start(X[:, 2 * i:2 * i + 2, :], A["xT"][:, 2 * i:2 * i + 2, :]), s_x[i])
        x_tok[2 * i] = x_tok[2 * i + 1] = t
    W.fill()

    sq = [at(f"sq{i}", [1024], O_V + (48 + 4 * i) * KB) for i in range(2)]
    dg = at("dg", [8, P], O_V + 56 * KB)
    tmp = [at(f"tmp{i}", [1024], O_V + 4 * i * KB) for i in range(2)]
    tmp_free = [None, None]
    U = pair("U", [8, 1024], O_U, O_U + 32 * KB)

    def apply_norm(rb, rtok, gain, x, dst, xtok, dst_free, n=8, shift=None, width=1024):
        toks, r = [], psum[:, rb:rb + 2, :].rearrange("p b n -> p (b n)")[:, 0:width]
        res = [None] * n

        def low(k):
            sh = None if shift is None else shift[:, k:k + 1]
            res[k] = part(tmp[k % 2][:, 0:width], *dst(k), toks[k], dst_free, bias=sh, q=pool if k % 3 == 1 else dve)
            tmp_free[k % 2] = res[k]

        for k in range(n + 1):
            if k < n:
                toks.append(dve.do(lambda e, k=k: e.scalar_tensor_tensor(
                    tmp[k % 2][:, 0:width], x(k), gain[:, k:k + 1], r, ALU.mult, ALU.mult),
                    xtok[k], rtok, tmp_free[k % 2]))
            if k > 0:
                low(k - 1)
        return res, toks[-1]

    nm = Norm(INV1024, T, sq + [at("sq2", [1024], O_V + 56 * KB)])
    for k in range(8):
        nm.add(X[:, k, :], x_tok[k], last=k == 7)
    W.prepare(2)
    rb, rn, rtok = nm.finish(dg, nm.total, 0)
    u_tok, a = apply_norm(rb, rtok, G1, lambda k: X[:, k, :], lambda k: (U[0][:, k, :], U[1][:, k, :]), x_tok, None)
    done(rb, rn, a)
    x_dead = a

    def ch(t, k, c0=0, c1=1024):
        return (t[0][:, k, c0:c1], t[1][:, k, c0:c1])

    def wt(tile, kc, n):
        return tile[0][:, kc * n:(kc + 1) * n], tile[1][:, kc * n:(kc + 1) * n]

    def proj_T(act_t, toks, nk=8, halves=((0, 512), (512, 1024)), base_k=0, n_w=128, sub=0, tile=None):
        res = []
        own = tile is None
        if own:
            tile = W.take()
        for c0, c1 in halves:
            b = banks(1)
            for k in range(nk):
                l = (tile[0][:, k * n_w + sub:k * n_w + sub + 128], tile[1][:, k * n_w + sub:k * n_w + sub + 128])
                mm3(psum[:, b, 0:c1 - c0], l, ch(act_t, k, c0, c1), k == 0, k == nk - 1, (tile[2], toks[k]))
            res.append((b, pe.mark()))
        if own:
            W.release(tile[3], res[-1][1])
        return res

    def banks_but(avoid, n):
        held.update(avoid)
        r = [banks(1) for _ in range(n)]
        held.difference_update(avoid)
        return r

    def proj_first(act_t, toks, n, avoid):
        tiles = [W.take() for _ in range(n)]
        bs = banks_but(avoid, 2 * n)
        bs = [bs[2 * i:2 * i + 2] for i in range(n)]
        for k in range(8):
            for tile, bb in zip(tiles, bs):
                for i, b in enumerate(bb):
                    mm3(psum[:, b, :], wt(tile, k, 128), ch(act_t, k, 512 * i, 512 * i + 512), k == 0, k == 7,
                        (tile[2], toks[k]))
        m = pe.mark()
        for tile in tiles:
            W.release(tile[3], m)
        return [[(b, m) for b in bb] for bb in bs]

    kT = pair("kT", [1024], O_V + 16 * KB, O_V + 20 * KB)
    vz = pair("vz", [8, 192], O_V + 24 * KB, O_V + 30 * KB)
    R = [at(f"R{i}", [1024], O_X + (8 + 4 * i) * KB) for i in range(2)]
    ones_r = at("ones_r", [128], O_V + 56 * KB, F32R)
    oz = at("oz", [192], O_V + 56 * KB + 512, F32R)
    mhl = at("mhl", [2, 64], O_V + 57 * KB + 256, F32R)
    ort = [dve.do(lambda e: e.memset(f(ones_r[:]), 1.0), nm.dg_done),
           dve.do(lambda e: e.memset(f(oz[:, 64:128]), 1.0)),
           dve.do(lambda e: e.memset(f(oz[:].rearrange("p (a d) -> p a d", d=64)[:, 0:3:2, :]), 0.0))]
    zt = [dve.do(lambda e, x=x: e.memset(f(vz[x][:, :, 64:128]), 1.0 - x), nm.m) for x in range(2)]
    kt_, vt = W.take(), W.take()
    kb_ = banks_but((rb, rb + 1), 4)
    kb_, vb_ = kb_[0:2], kb_[2:4]
    for k in range(8):
        for i in range(2):
            mm3(psum[:, kb_[i], :], wt(kt_, k, 128), ch(U, k, 512 * i, 512 * i + 512), k == 0, k == 7,
                (kt_[2], u_tok[k]))
        for i in range(2):
            mm3(psum[:, vb_[i], :], wt(vt, k, 128), ch(U, k, 512 * i, 512 * i + 512), k == 0, k == 7, (vt[2],))
    m = pe.mark()
    W.release(kt_[3], m)
    W.release(vt[3], m)
    kt_tok, v_tok = [], [zt]
    for i, b in enumerate(kb_):
        sl = slice(512 * i, 512 * i + 512)
        c = dve.do(lambda e, b=b, sl=sl: e.tensor_scalar(R[0][:, sl], bank(b), 0.125, None, ALU.mult), m, x_dead, nm.m)
        done(b, 1, c)
        kt_tok += part(R[0][:, sl], kT[0][:, sl], kT[1][:, sl], c, tmp_free)
    for q4, b in enumerate(vb_):
        sl = slice(512 * q4, 512 * q4 + 512)
        c = act.do(lambda e, b=b, sl=sl: e.activation(R[1][:, sl], bank(b), ACT.Copy), m, x_dead, nm.m)
        done(b, 1, c)
        b = banks(1)
        for n in range(4):
            pe.quiet(lambda e, b=b, n=n, q4=q4: e.transpose(
                psum[:, b, n * P:n * P + P], R[1][:, 512 * q4 + n * P:512 * q4 + n * P + P], ident[:]), c)
        mv_ = pe.mark()
        src = psum[:, b, :].rearrange("p (n h d) -> p n h d", n=4, h=2)
        d0, d1 = (vz[i][:, 4 * q4:4 * q4 + 4, :].rearrange("p n (a d) -> p n a d", d=64)[:, :, 0:3:2, :]
                  for i in range(2))
        hs = part(src, d0, d1, mv_)
        v_tok += hs
        done(b, 1, *hs)

    qb_ = [pair(f"q{i}", [1024], O_V + 8 * i * KB, O_V + (8 * i + 4) * KB) for i in range(2)]
    EX = [at(f"EX{i}", [512], O_V + (36 + 2 * i) * KB) for i in range(3)]
    EP = [pair(f"EP{i}", [512], O_V + (42 + 4 * i) * KB, O_V + (44 + 4 * i) * KB) for i in range(3)]
    Lj = [at(f"Lj{i}", [256], O_V + (54 + i) * KB) for i in range(2)]
    O_H2 = O_RING + (N_RAW * 4 + 16) * KB
    dgm = [pair(f"dgm{h}", [8, P], O_H2 + 8 * h * KB, O_H2 + (8 * h + 4) * KB) for h in range(2)]
    dge = pair("dge", [8, P], O_X, O_X + 4 * KB)
    Or = [at(f"Or{i}", [1024], O_X + (16 + 4 * i) * KB) for i in range(2)]
    bS = [at(f"bS{i}", [2, 256], O_X + (24 + 2 * i) * KB) for i in range(2)]
    bT = [at(f"bT{i}", [2, 256], O_X + (28 + 2 * i) * KB) for i in range(2)]
    old = [x_dead, nm.m, nm.dg_done, kt_tok, mv_]
    s_bias = [sem(f"s_bias{i}") for i in range(2)]
    s_os = [sem(f"s_os{i}") for i in range(2)]
    bias_free, bias_tok = [old, old], [None, None]
    q_free, q_tok = [tmp_free, tmp_free], [None, None]
    EX_free, EP_free, dgm_free, dge_free = [old] * 3, [old] * 3, [old] * 2, [old]
    R_free, Or_free, sm_free = [old] * 2, [old] * 2, [None, None]
    for i in range(8):
        pe.wait(free[i])
    A_free, B_free, O_free = [free[0], free[1]], [free[2], free[3]], [free[4:6], free[6:8]]
    O1 = U
    Oraw = at("Oraw", [8, 1024], O_U + 32 * KB)
    o_tok = [None] * 8
    Lj_tok, nL = [old, old], [0]
    mx_tok, dgm_tok, dge_tok, ex_tok, ep_tok, spill_tok, R_tok, Or_tok = {}, {}, {}, {}, {}, {}, {}, {}
    u_last = [None]

    def sv(s, i):
        return small[:, 64 * s + 16 * i:64 * s + 16 * i + 16]

    def nh(v):
        return v.rearrange("p (n h) -> p n h", h=2)

    def load_bias(j):
        i = j % 2
        pool.dma(lambda e: e.dma_start(bS[i][:], A["bias"][j]), s_bias[i], bias_free[i])
        bias_tok[i] = pool.dma(lambda e: e.dma_start(bT[i][:], A["bias_t"][j]), s_bias[i])

    q_tile = {}

    def q_proj(j, i):
        if i == 0:
            q_tile[j] = W.take()
            q_tok[j % 2] = []
        tile, sl = q_tile[j], slice(512 * i, 512 * i + 512)
        pe.wait(A_free[i])
        for k in range(8):
            mm3(psum[:, i, :], wt(tile, k, 128), ch(U, k, 512 * i, 512 * i + 512), k == 0, k == 7, (tile[2], u_tok[k]))
        m = pe.mark()
        p = part(psum[:, i, :], qb_[j % 2][0][:, sl], qb_[j % 2][1][:, sl], m, q_free[j % 2])
        A_free[i] = p
        q_tok[j % 2] += p
        if i == 1:
            W.release(tile[3], m)
            u_last[0] = m

    def chunk(j, c):
        s, q = j % 2, qb_[j % 2]
        pe.wait(A_free)
        for n in (2 * c, 2 * c + 1):
            lo = 0 if n == 0 else (n - 1) * P
            w, c1 = (n + 1) * P - lo, 256 * (n % 2) + 256
            for x, y in ((0, 0), (1, 0), (0, 1)):
                for h in range(2):
                    pr = slice(64 * h, 64 * h + 64)
                    mm(psum[:, h, c1 - w:c1], q[x][pr, n * P:(n + 1) * P], kT[y][pr, lo:lo + w],
                       (x, y) == (0, 0), (x, y) == (0, 1), (q_tok[s], kt_tok))
        m = pe.mark()
        for h in range(2):
            for n in (2 * c, 2 * c + 1):
                w = 128 if n == 0 else 256
                c1, i, z = 256 * (n % 2) + 256, 2 * n + h, nL[0] % 2
                nL[0] += 1
                Lj_tok[z] = dve.do(lambda e, h=h, i=i, w=w, c1=c1, z=z: e.tensor_tensor_reduce(
                    Lj[z][:, 256 - w:256], psum[:, h, c1 - w:c1], bS[s][:, h, 256 - w:256], 1.0, -3.0e38,
                    ALU.add, ALU.max, sv(s, 0)[:, i:i + 1]), m, bias_tok[s], sm_free[s], Lj_tok[z])
            A_free[h] = Lj_tok[z]
        mx_tok[j] = Lj_tok[z]

    def max_diag(j):
        s = j % 2
        sk = SINK[:, 2 * j:2 * j + 2].unsqueeze(1).to_broadcast([P, 8, 2])
        hl_ = [mhl[:, s, 16 * i:16 * i + 16] for i in range(4)]
        a = dve.do(lambda e: e.tensor_tensor(nh(sv(s, 1)), nh(sv(s, 0)), sk, ALU.max), mx_tok[j], sm_free[s])
        a2 = dve.do(lambda e: e.tensor_scalar(sv(s, 0), sv(s, 1), -1.0, None, ALU.mult), a)
        a3 = dve.do(lambda e: e.tensor_tensor(nh(sv(s, 2)), sk, nh(sv(s, 1)), ALU.subtract), a)
        p = part(sv(s, 0), hl_[0], hl_[1], a2, sm_free[s])
        es = act.do(lambda e: e.activation(sv(s, 3), sv(s, 2), ACT.Exp), a3)
        pe_ = part(sv(s, 3), hl_[2], hl_[3], es, sm_free[s])
        sm_free[s] = []
        sm_free[s] = pe_
        dge_tok[j], mhl_tok[j] = pe_, p

    def diag(j, h):
        s = j % 2
        dgm_tok[j, h] = []
        for x in range(2):
            t = dve.do(lambda e, x=x: e.tensor_tensor(
                dgm[h][x][:], ident[:, None, :].to_broadcast([P, 8, P]),
                f(nh(mhl[:, s, 16 * x:16 * x + 16])[:, :, h]).unsqueeze(2).to_broadcast([P, 8, P]),
                ALU.mult), mhl_tok[j], dgm_free[h])
            dgm_tok[j, h].append(t)
        sm_free[s] = sm_free[s] + [t]

    def sink_diag(j, h):
        s = j % 2
        r = []
        for x in range(2):
            r.append(pool.do(lambda e, x=x: e.tensor_tensor(
                dge[x][:], ident[:, None, :].to_broadcast([P, 8, P]),
                f(nh(mhl[:, s, 32 + 16 * x:48 + 16 * x])[:, :, h]).unsqueeze(2).to_broadcast([P, 8, P]),
                ALU.mult), dge_tok[j], dge_free[0]))
        sm_free[s] = sm_free[s] + [r[-1]]
        dge_tok[j, h] = r

    mhl_tok = {}
    units = [(j, h, p) for j in range(8) for h in range(2) for p in range(4)]

    def logits(u):
        j, h, p = units[u]
        r, q, pr = 2 + u % 2, qb_[j % 2], slice(64 * h, 64 * h + 64)
        pe.wait(B_free[u % 2])
        for i in range(2):
            kb = 2 * p + i
            w = 256 if kb < 7 else 128
            o = psum[:, r, 256 * i:256 * i + w]
            mm3(o, [kT[x][pr, kb * P:kb * P + P] for x in range(2)], [q[x][pr, kb * P:kb * P + w] for x in range(2)],
                True, False, (q_tok[j % 2], kt_tok))
            for x in range(2):
                mm(o, ones_r[:], dgm[h][x][:].rearrange("p a b -> p (a b)")[:, kb * P:kb * P + w],
                   False, x == 1, (dgm_tok[j, h], ort))
        m = pe.mark()
        if p == 3:
            dgm_free[h] = m
            if h == 1:
                q_free[j % 2] = m
        v = lambda y: y.rearrange("p (i q) -> p i q", i=2)
        t = []
        for i0, i1, w in ((0, 2, 256),) if p < 3 else ((0, 1, 256), (1, 2, 128)):
            t.append(dve.do(lambda e, i0=i0, i1=i1, w=w: e.tensor_tensor(
                v(EX[u % 3][:])[:, i0:i1, 0:w], v(bank(r))[:, i0:i1, 0:w],
                bT[j % 2][:, h:h + 1, 0:w].to_broadcast([P, i1 - i0, w]), ALU.add), m, bias_tok[j % 2], EX_free[u % 3]))
        B_free[u % 2] = t
        if h == 1 and p == 3:
            bias_free[j % 2] = t
        w = 512 if p < 3 else 384
        ex_tok[u] = act.do(lambda e: e.activation(EX[u % 3][:, 0:w], EX[u % 3][:, 0:w], ACT.Exp), t)

    def split(u):
        w = 512 if units[u][2] < 3 else 384
        ep_tok[u] = part(EX[u % 3][:, 0:w], EP[u % 3][0][:, 0:w], EP[u % 3][1][:, 0:w], ex_tok[u], EP_free[u % 3])
        EX_free[u % 3] = ep_tok[u]

    def times_v(u):
        j, h, p = units[u]
        if p == 0:
            pe.wait(O_free[h])
            for b in range(2):
                for x in range(2):
                    mm(psum[:, 4 + 2 * h + b, :], oz[:, 64 * h:64 * h + 128],
                       dge[x][:].rearrange("p a b -> p (a b)")[:, 512 * b:512 * b + 512],
                       x == 0, False, (dge_tok[j, h],), True)
            dge_free[0] = pe.mark()
        for i in range(2):
            kb = 2 * p + i
            l = [vz[x][:, kb, 64 * h:64 * h + 128] for x in range(2)]
            spans = ((0, 256),) if kb not in (3, 7) else ((0, 128), (128, 256)) if kb == 3 else ((0, 128),)
            for c0, c1 in spans:
                q0 = kb * P + c0
                o = psum[:, 4 + 2 * h + q0 // 512, q0 % 512:q0 % 512 + c1 - c0]
                r = [EP[u % 3][x][:, 256 * i + c0:256 * i + c1] for x in range(2)]
                last = (kb, c0) in ((3, 0), (7, 0))
                for n, (x, y) in enumerate(((0, 0), (1, 0), (0, 1))):
                    mm(o, l[x], r[y], False, last and n == 2, (ep_tok[u], v_tok), True)
        EP_free[u % 3] = m = pe.mark()
        if p == 3:
            r0, s0, z = 64 * h, 64 * (1 - h), j % 2
            o = two(4 + 2 * h)
            a = act.do(lambda e: e.activation(Or[z][r0:r0 + 64, :], o[r0:r0 + 64, :], ACT.Copy), m, Or_free[z])
            d = dve.do(lambda e: e.tensor_copy(R[z][r0:r0 + 64, :], o[s0:s0 + 64, :]), m, R_free[z])
            O_free[h] = [a, d]
            R_tok.setdefault(j, []).append(d)
            Or_tok.setdefault(j, []).append(a)

    def invert(j, c):
        sl, z = slice(256 * c, 256 * c + 256), j % 2
        R_tok[j, c] = dve.do(lambda e: e.reciprocal(R[z][:, sl], R[z][:, sl]), R_tok[j])

    def scale(j, c0, c1, q):
        z, sl = j % 2, slice(256 * c0, 256 * c1)
        tk = [R_tok[j, c] for c in range(c0, c1)] + Or_tok[j]
        dst = Or[z][:, sl] if j < 6 else Oraw[:, j, sl]
        t = q.do(lambda e: e.tensor_tensor(dst, Or[z][:, sl], R[z][:, sl], ALU.mult), tk, u_last[0] if j >= 6 else None)
        R_free[z], Or_free[z] = t, t
        if j < 6:
            spill_tok[j] = Or_free[z] = pool.dma(lambda e: e.dma_start(A["os"][j], Or[z][:]), s_os[z], t)
        else:
            o_tok[j] = (o_tok[j] or []) + join(j, t, sl)

    def join(j, t, sl=slice(0, 1024)):
        return part(Oraw[:, j, sl], O1[0][:, j, sl], O1[1][:, j, sl], t, u_last[0])

    s_or = sem("s_or")

    def reload(j):
        spill_tok[j] = pool.dma(lambda e: e.dma_start(Oraw[:, j, :], A["os"][j]), s_or, spill_tok[j], u_last[0])

    for j in range(2):
        load_bias(j)
        q_proj(j, 0)
        q_proj(j, 1)
    for c in range(4):
        chunk(0, c)
    max_diag(0)
    diag(0, 0)
    diag(0, 1)
    sink_diag(0, 0)
    logits(0)
    logits(1)
    split(0)
    for u in range(64):
        if u + 1 < 64:
            split(u + 1)
        if u + 2 < 64:
            logits(u + 2)
        j, i = u // 8, u % 8
        times_v(u)
        if i == 0:
            sink_diag(j, 1)
        if i == 4 and j < 7:
            max_diag(j + 1)
            diag(j + 1, 0)
            sink_diag(j + 1, 0)
        if i == 5 and j < 7:
            diag(j + 1, 1)
        if i < 4:
            if j < 7:
                chunk(j + 1, i)
            if j > 0:
                invert(j - 1, i)
                if i == 3:
                    scale(j - 1, 0, 4, pool)
        if i >= 6 and j < 6:
            q_proj(j + 2, i - 6)
        if i == 6 and j < 6:
            load_bias(j + 2)
        if j == 7 and i >= 1:
            if i == 1:
                for n in range(6):
                    reload(n)
            if i <= 6:
                o_tok[i - 1] = join(i - 1, (s_or, 16 * 6))
    for c in range(4):
        invert(7, c)
        scale(7, c, c + 1, dve)
    m_att = EP_free[63 % 3]
    osplit = [t for j in range(8) for t in o_tok[j]]
    for i in range(2):
        free[i], free[2 + i], free[4 + i], free[6 + i] = A_free[i], B_free[i], O_free[0], O_free[1]
    W.lend([2, 3], m_att)

    s_x2 = [sem(f"s_xr{i}") for i in range(4)]
    for i in range(4):
        t = pool.dma(lambda e, i=i: e.dma_start(X[:, 2 * i:2 * i + 2, :], A["xT"][:, 2 * i:2 * i + 2, :]),
                     s_x2[i], m_att, osplit)
        x_tok[2 * i] = x_tok[2 * i + 1] = t

    nm = Norm(INV1024, T, sq, osplit)
    for n in range(8):
        res = proj_T(O1, o_tok)
        ts = []
        for i, (b, m) in enumerate(res):
            sl = slice(512 * i, 512 * i + 512)
            t = dve.do(lambda e, b=b, sl=sl, n=n: e.tensor_tensor(X[:, n, sl], bank(b), X[:, n, sl], ALU.add),
                       m, x_tok[n])
            done(b, 1, t)
            ts.append(t)
        x_tok[n] = ts
        nm.add(X[:, n, :], ts, last=n == 7)
    u_dead = m
    rb, rn, rtok = nm.finish(dg, osplit, 0)
    mraw = [at(f"mraw{i}", [512], O_V + (48 + 2 * i) * KB) for i in range(2)]
    srow = at("srow", [1024], O_V + 52 * KB)
    s_m = [sem(f"s_m{i}") for i in range(2)]
    m_free = [nm.sqf, nm.sqf]
    s_s = sem("s_srow")
    s_state = {"tok": None, "free": nm.sqf}
    mod_jobs = [(0, i) for i in range(96)] + [(1, i) for i in range(32)]
    mod_ld = {}

    def row_load(name):
        return pool.dma(lambda e: e.dma_start(srow[:], A[name]), s_s, s_state["free"])

    def row_silu(t):
        s_state["tok"] = act.do(lambda e: e.activation(srow[:], srow[:], ACT.Silu), t)

    def mod_load(n):
        if n < 128:
            i = mod_jobs[n][1]
            mod_ld[n] = pool.dma(lambda e: e.dma_start(mraw[n % 2][:], A["w_mod"][i]), s_m[n % 2], m_free[n % 2])

    def mod_step(n):
        who, i = mod_jobs[n]
        if n == 96:
            row_silu(row_load("cc_b"))
        c = 48 * who + i // 2
        dst = (modb if i % 2 else mod)[:, c:c + 1]
        t = dve.do(lambda e: e.tensor_tensor_reduce(mraw[n % 2][:], mraw[n % 2][:],
                                                    srow[:, 512 * (i % 2):512 * (i % 2) + 512], 1.0, 0.0,
                                                    ALU.mult, ALU.add, dst),
                   mod_ld[n], s_state["tok"])
        m_free[n % 2] = t
        s_state["free"] = t
        mod_load(n + 2)

    mod_load(0)
    mod_load(1)
    c_row = row_load("c_b")
    for i in range(2):
        tmp_free[i] = [tmp_free[i], m_att]
    u_tok, a = apply_norm(rb, rtok, G2, lambda k: X[:, k, :], lambda k: ch(U, k), x_tok, u_dead)
    done(rb, rn, a)

    row_silu(c_row)

    NA = 6
    ab = [pair(f"a{i}", [1024], O_V + 8 * i * KB, O_V + (8 * i + 4) * KB) for i in range(NA)]
    a_free = [[u_tok, m_att] for _ in range(NA)]
    a_tok = {}
    relu = [at(f"relu{i}", [512], O_V + (56 + 2 * i) * KB) for i in range(2)]
    r_free = [nm.dg_done, nm.dg_done]
    ri = [0]
    ahead = {}

    def up(i):
        s = i % NA
        toks = []
        if i == 0:
            ahead.update(enumerate(proj_first(U, u_tok, 3, (rb, rb + 1))))
        for hfi, (b, m) in enumerate(ahead.pop(i) if i in ahead else proj_T(U, u_tok)):
            sl = slice(512 * hfi, 512 * hfi + 512)
            rr, rf = relu[ri[0] % 2], ri[0] % 2
            ri[0] += 1
            t1 = act.do(lambda e, rr=rr, b=b: e.activation(rr[:], bank(b), ACT.Relu), m, r_free[rf])
            done(b, 1, t1)
            t2 = act.do(lambda e, rr=rr, s=s, sl=sl: e.activation(ab[s][0][:, sl], rr[:], ACT.Square), t1, a_free[s])
            t3 = dve.do(lambda e, rr=rr: e.tensor_tensor(rr[:], rr[:], rr[:], ALU.mult), t1, t2)
            t4 = dve.do(lambda e, rr=rr, s=s, sl=sl: e.tensor_tensor(
                ab[s][1][:, sl], rr[:], f(ab[s][0][:, sl]), ALU.subtract), t2, t3, a_free[s])
            r_free[rf] = t4
            toks += [t2, t4]
        a_tok[i] = toks

    def down(g, last):
        for q4 in range(4):
            tile = W.take()
            for n in (2 * q4, 2 * q4 + 1):
                ts = []
                for hfi in range(2):
                    b = banks(1)
                    for c in range(4):
                        i = 4 * g + c
                        l = [tile[x][:, c * 256 + (n % 2) * 128:c * 256 + (n % 2) * 128 + 128] for x in range(2)]
                        r = [ab[i % NA][x][:, 512 * hfi:512 * hfi + 512] for x in range(2)]
                        mm3(psum[:, b, :], l, r, c == 0, c == 3, (tile[2], a_tok[i]))
                    m = pe.mark()
                    sl = slice(512 * hfi, 512 * hfi + 512)
                    t = dve.do(lambda e, b=b, n=n, sl=sl: e.tensor_tensor(
                        X[:, n, sl], bank(b), X[:, n, sl], ALU.add), m, x_tok[n], u_tok)
                    done(b, 1, t)
                    ts.append(t)
                x_tok[n] = ts
                if last:
                    nm.add(X[:, n, :], ts)
                    nmg.add(X[:, n, :], ts, scale=GF[:, n:n + 1])
            W.release(tile[3], m)
        for c in range(4):
            a_free[(4 * g + c) % NA] = m

    nx, jobs = 0, 0

    def ups(n):
        nonlocal nx, jobs
        for _ in range(n):
            if nx < 32:
                up(nx)
                nx += 1
                if nx >= 6:
                    for _ in range(5):
                        if jobs < 128:
                            mod_step(jobs)
                            jobs += 1
    ups(6)
    for g in range(8):
        last = g == 7
        if last:
            assert jobs == 128
            nm = Norm(INV1024, T, sq, [m_free, s_state["free"]])
            nmg = Norm(INV1024, T, [at(f"sqg{i}", [1024], O_V + (16 + 4 * i) * KB) for i in range(2)], a_free[2])
            dgg_free = a_free[3]
        down(g, last)
        ups(4)
    m0 = dve.do(lambda e: e.tensor_tensor(mod[:], mod[:], modb[:], ALU.add), m_free)
    mt = dve.do(lambda e: e.tensor_tensor(mod[:, 0:48], mod[:, 0:48], BMOD, ALU.add), m0)
    mt2 = dve.do(lambda e: e.tensor_tensor(mod[:, 48:64], mod[:, 48:64], BMOD[:, 0:16], ALU.add), m0)
    t1 = dve.do(lambda e: e.scalar_tensor_tensor(mod[:, 8:16], mod[:, 8:16], 1.0, N1, ALU.add, ALU.mult), mt)
    t2 = dve.do(lambda e: e.scalar_tensor_tensor(mod[:, 32:40], mod[:, 32:40], 1.0, N2, ALU.add, ALU.mult), mt)
    t3 = dve.do(lambda e: e.scalar_tensor_tensor(mod[:, 56:64], mod[:, 56:64], 1.0, N1, ALU.add, ALU.mult), mt2)
    mod_tok = [t1, t2, t3]
    SH1, SC1, GT1 = mod[:, 0:8], mod[:, 8:16], mod[:, 16:24]
    SH2, SC2, GT2 = mod[:, 24:32], mod[:, 32:40], mod[:, 40:48]
    CSH1, CSC1 = mod[:, 48:56], mod[:, 56:64]

    s_sp = [sem(f"s_spill{i}") for i in range(4)]
    spilled = [None] * 4
    dgg = at("dgg", [8, P], O_V + 24 * KB)
    b = banks(1)
    for o, z in ((0, nm), (8, nmg)):
        for tb in range(8):
            mm(psum[:, b, o + tb:o + tb + 1], z.sq[0][:, tb * P:(tb + 1) * P], INV1024,
               (o, tb) == (0, 0), (o, tb) == (8, 7), (z.total,), True)
    sq_dead = pe.mark()
    s1, s2, r1, r2, r12, ms = st[:, 0, 0:8], st[:, 0, 8:16], st[:, 1, 0:8], st[:, 1, 8:16], st[:, 2, 0:8], st[:, 3, 0:8]
    SCF = modb[:, 0:8]
    scf = dve.do(lambda e: e.tensor_tensor(SCF, SC1, GF, ALU.mult), mod_tok, m0)
    t = act.do(lambda e, b=b: e.activation(s1, psum[:, b, 0:8], ACT.Sqrt, bias=EPSV), sq_dead, rs_free[0])
    t1 = dve.do(lambda e: e.reciprocal(r1, s1), t, rs_free[0])
    t2 = dve.do(lambda e, b=b: e.tensor_tensor(ms, psum[:, b, 8:16], r1, ALU.mult), t1, sq_dead)
    done(b, 1, t, t2)
    t2 = dve.do(lambda e: e.tensor_tensor(ms, ms, r1, ALU.mult), t2)
    t = act.do(lambda e: e.activation(s2, ms, ACT.Sqrt, bias=EPSV), t2)
    t = dve.do(lambda e: e.reciprocal(r2, s2), t)
    t = dve.do(lambda e: e.tensor_tensor(r12, r1, r2, ALU.mult), t)
    rbs = []
    for g_, r_, fr in ((dg, r12, [r_free, sq_dead]), (dgg, r1, dgg_free)):
        t = dve.do(lambda e, g_=g_, r_=r_: e.tensor_tensor(
            g_[:], ident[:, None, :].to_broadcast([P, 8, P]), r_.unsqueeze(2).to_broadcast([P, 8, P]), ALU.mult),
            t, t1, fr)
        b = banks(2)
        for i in range(2):
            mm(psum[:, b + i, :], ones[:], g_[:, 4 * i:4 * i + 4, :].rearrange("p a b -> p (a b)"), True, True, (t,))
        rbs.append((b, pe.mark()))
    rs_free[0] = [t]
    (rb, rtok), (rb1, rtok1) = rbs
    a_dead = sq_dead
    dg_dead = rtok
    tmp_free = [a_dead, a_dead]
    u_tok, a = apply_norm(rb, rtok, SCF, lambda k: X[:, k, :], lambda k: ch(U, k),
                          [[x_tok[k], scf, mod_tok] for k in range(8)], a_dead, shift=SH1)
    done(rb, 2, a)
    held.update((rb1, rb1 + 1))

    def spill_x1(g):
        for k in (2 * g, 2 * g + 1):
            t = dve.do(lambda e, k=k: e.scalar_tensor_tensor(
                X[:, k, :], X[:, k, :], GF[:, k:k + 1], two(rb1), ALU.mult, ALU.mult), rtok1, a)
            x_tok[k] = t
            spilled[g] = pool.dma(lambda e, k=k: e.dma_start(A["x1s"][:, k, :], X[:, k, :]), s_sp[g], t)
        if g == 3:
            done(rb1, 2, t)
            held.difference_update((rb1, rb1 + 1))

    fT = pair("fT", [1024], O_V, O_V + 4 * KB)
    Zh = at("Z_hi", [4, 8, 256], O_X, F32R)
    Zl = at("Z_lo", [4, 8, 256], O_V + 8 * KB, F32R)
    cdr = at("cdr", [256], O_V + 42 * KB)
    cdp = pair("cd", [256], O_V + 40 * KB, O_V + 41 * KB)
    s_cd = sem("s_cd")
    t = pool.dma(lambda e: e.dma_start(cdr[:], A["dft_c"]), s_cd, a_dead)
    cd = (cdp[0], cdp[1], part(cdr[:], cdp[0][:], cdp[1][:], t, a_dead))
    f_free = tmp_free
    ahead.update(enumerate(proj_first(U, u_tok, 2, (rb, rb + 1, rb1, rb1 + 1))))
    for g in range(4):
        ft = []
        for i, (b, m) in enumerate(ahead.pop(g) if g in ahead else proj_T(U, u_tok)):
            sl = slice(512 * i, 512 * i + 512)
            p = part(bank(b), fT[0][:, sl], fT[1][:, sl], m, f_free)
            done(b, 1, *p)
            ft.append(p)
        if g == 0:
            for i in range(4):
                spill_x1(i)
        for n2 in range(4):
            b = banks(1)
            for i in range(2):
                n = 2 * n2 + i
                l = (fT[0][:, n * P:n * P + P], fT[1][:, n * P:n * P + P])
                mm3(psum[:, b, 256 * i:256 * i + 256], l, (cd[0][:, 0:256], cd[1][:, 0:256]),
                    True, True, (ft[n // 4], cd[2]))
            m = pe.mark()
            z0, z1 = (z[:, g, 2 * n2:2 * n2 + 2, :].rearrange("p a b -> p (a b)") for z in (Zh, Zl))
            p = part(bank(b), z0, z1, m, [spilled[g], rtok1, a_dead])
            done(b, 1, *p)
            z_tok = p
        f_free = m
    turn[0] = 0
    banks(8)
    for c in range(16):
        tile = W.take()
        for g in range(4):
            n, cs = c % 8, c // 8
            l = tuple(z[:, g, n, 128 * cs:128 * cs + 128] for z in (Zh, Zl))
            for i in range(2):
                r = (tile[0][:, 512 * i:512 * i + 512], tile[1][:, 512 * i:512 * i + 512])
                mm3(psum[:, 2 * g + i, :], l, r, c == 0, c == 15, (tile[2], z_tok))
        m = pe.mark()
        W.release(tile[3], m)
    z_dead = m
    Y = pair("Y", [4, 1024], O_X, O_X + 16 * KB)
    y_tok = []
    for g in range(4):
        yt = []
        for i in range(2):
            sl = slice(512 * i, 512 * i + 512)
            p = part(bank(2 * g + i), Y[0][:, g, sl], Y[1][:, g, sl], m)
            done(2 * g + i, 1, *p)
            yt += p
        y_tok.append(yt)
    cT = at("cT", [8, 256], O_V + 8 * KB)
    HC = pair("HC", [8, 256], O_V + 16 * KB, O_V + 24 * KB)
    csq = [at(f"csq{i}", [256], O_V + (32 + i) * KB) for i in range(2)]
    ctmp = [at(f"ctmp{i}", [256], O_V + (34 + i) * KB) for i in range(2)]
    cdg = at("cdg", [2, P], O_V + 36 * KB)
    s_ct = sem("s_ctx")
    ct_tok = pool.dma(lambda e: e.dma_start(cT[:], A["ctxT"]), s_ct, z_dead)
    gbs = [at(f"gb{i}", [1024], O_V + (40 + 4 * i) * KB) for i in range(2)]
    tsb = [at(f"tsb{i}", [1024], O_V + (48 + 4 * i) * KB) for i in range(2)]
    s_ts = [sem(f"s_ts{i}") for i in range(2)]
    g_free, t_free = [sq_dead, sq_dead], [sq_dead, dg_dead]
    hc_tok = [None] * 8
    ctx_end = []

    def context():
        cn = Norm(INV1024, TC, csq, z_dead)
        for k in range(8):
            cn.add(cT[:, k, :], ct_tok, last=k == 7)
        rb, rn, rtok = cn.finish(cdg, z_dead, 0)
        fr = [z_dead, z_dead]
        for k in range(8):
            a = dve.do(lambda e, k=k, r=bank(rb, 0, 256): e.scalar_tensor_tensor(
                ctmp[k % 2][:], cT[:, k, :], CSC1[:, k:k + 1], r, ALU.mult, ALU.mult), rtok, ct_tok, mod_tok, fr[k % 2])
            hc_tok[k] = part(ctmp[k % 2][:], HC[0][:, k, :], HC[1][:, k, :], a, z_dead, bias=CSH1[:, k:k + 1])
            fr[k % 2] = hc_tok[k]
        done(rb, rn, a)
        ctx_end.append([fr, cn.sqf, cn.dg_done])

    for j in range(8):
        if j == 1:
            context()
        gt, tt = gbs[j % 2], tsb[j % 2]
        ga_ = []
        for i, (b, m) in enumerate(proj_T(U, u_tok)):
            sl = slice(512 * i, 512 * i + 512)
            t = act.do(lambda e, b=b, sl=sl, gt=gt: e.activation(gt[:, sl], bank(b), ACT.Sigmoid), m, g_free[j % 2])
            done(b, 1, t)
            ga_.append(t)
        if j % 2 == 0:
            fo_tile = W.take()
        for i, (b, m) in enumerate(proj_T(Y, y_tok, nk=4, n_w=256, sub=128 * (j % 2), tile=fo_tile)):
            sl = slice(512 * i, 512 * i + 512)
            t = dve.do(lambda e, b=b, sl=sl, gt=gt, tt=tt: e.tensor_tensor(tt[:, sl], bank(b), gt[:, sl], ALU.mult),
                       m, ga_, t_free[j % 2])
            done(b, 1, t)
        if j % 2 == 1:
            W.release(fo_tile[3], m)
        g_free[j % 2] = t
        t_free[j % 2] = pool.dma(lambda e, j=j, tt=tt: e.dma_start(A["ts"][j], tt[:]), s_ts[j % 2], t)
    y_dead = m

    cqr = at("cqr", [3, 1024], O_X)
    ckr = at("ckr", [2, TA], O_X + 12 * KB)
    kpe = at("kpe", [10, 32], O_X + 30 * KB)
    cq = pair("cq", [3, 1024], O_V + 32 * KB, O_V + 44 * KB)
    ck = pair("ck", [2, TA], O_V + 8 * KB, O_V + 18 * KB)
    sq3 = [at(f"sq3_{i}", [1024], O_X + (22 + 4 * i) * KB) for i in range(2)]
    dg3 = at("dg3", [8, P], O_V + 28 * KB)
    gas = [at("gas0", [1024], O_X + 24 * KB), at("gas1", [1024], O_V + 56 * KB),
           at("gas2", [1024], O_V), at("gas3", [1024], O_V + 4 * KB)]
    s_ga = [sem(f"s_ga{i}") for i in range(4)]
    ga_free = [None] * 4

    n_q = Norm(INV384, T, sq3, y_dead)
    for k in range(3):
        ts = []
        for i, (b, m) in enumerate(proj_T(U, u_tok)):
            sl = slice(512 * i, 512 * i + 512)
            t = dve.do(lambda e, b=b, k=k, sl=sl: e.tensor_copy(cqr[:, k, sl], bank(b)), m, y_dead)
            done(b, 1, t)
            ts.append(t)
        n_q.add(cqr[:, k, :], ts, last=k == 2)
    cq_t = ts
    n_k = Norm(INV256, T, [sq3[0]], n_q.sqf)
    n_c = Norm(INV256, TC, [sq3[1]], n_q.sqf)
    for k in range(2):
        ts = []
        tile = W.take()
        res = proj_T(U, u_tok, tile=tile) + proj_T(HC, hc_tok, halves=((0, 256),), tile=tile)
        W.release(tile[3], res[-1][1])
        for i, (b, m) in enumerate(res):
            w = 512 if i < 2 else 256
            t = dve.do(lambda e, b=b, k=k, i=i, w=w: e.tensor_copy(ckr[:, k, 512 * i:512 * i + w], bank(b, 0, w)),
                       m, y_dead)
            done(b, 1, t)
            ts.append(t)
        n_k.add(ckr[:, k, 0:T], ts, last=k == 1)
        n_c.add(ckr[:, k, T:TA], ts, last=k == 1)
    ck_t = ts
    tile = W.take()
    kpT = at("kpT", [TA], O_V)
    kp_t = []
    for src, c0, w, o in ((U, 0, 512, 0), (U, 512, 512, 512), (HC, 0, 256, 1024)):
        b = banks(1)
        for k in range(8):
            mm3(psum[0:32, b, 0:w], wt(tile, k, 32), ch(src, k, c0, c0 + w), k == 0, k == 7, (tile[2], hc_tok))
        kp_t.append(act.do(lambda e, b=b, w=w, o=o: e.activation(kpT[0:32, o:o + w], psum[0:32, b, 0:w], ACT.Copy),
                           pe.mark(), f_free))
        done(b, 1, kp_t[-1])
    W.release(tile[3], pe.mark())
    b = banks(1)
    for n in range(10):
        pe.quiet(lambda e, b=b, n=n: e.transpose(
            psum[:, b, 32 * n:32 * n + 32], kpT[0:32, n * P:n * P + P], ident[0:32, 0:32]), kp_t)
    hc_dead = pe.mark()
    kpe_tok = dve.do(lambda e, b=b: e.tensor_copy(kpe[:].rearrange("p a b -> p (a b)"), bank(b, 0, 320)),
                     hc_dead, y_dead)
    done(b, 1, kpe_tok)

    def ga_block(j):
        s = j % 2 if j < 3 else 2 + j % 2
        gt = gas[s]
        for i, (b, m) in enumerate(proj_T(U, u_tok)):
            sl = slice(512 * i, 512 * i + 512)
            t = act.do(lambda e, b=b, sl=sl: e.activation(gt[:, sl], bank(b), ACT.Sigmoid), m, ga_free[s])
            done(b, 1, t)
        ga_free[s] = pool.dma(lambda e: e.dma_start(A["gas"][j], gt[:]), s_ga[s], t)
        return m

    rb, rn, rtok = n_q.finish(dg3, hc_dead, 0)
    old = [ctx_end, t_free, g_free, sq_dead]
    tmp_free = [[f_free, hc_dead], [f_free, hc_dead]]
    cq_tok, a = apply_norm(rb, rtok, GQA, lambda k: cqr[:, k, :], lambda k: ch(cq, k), [cq_t] * 3, old, n=3)
    done(rb, rn, a)
    cqr_dead = a
    rb, rn, rtok = n_k.finish(dg3, n_q.dg_done, 2)
    ck_tok, a = apply_norm(rb, rtok, GKVA, lambda k: ckr[:, k, 0:T], lambda k: ch(ck, k, 0, T), [ck_t] * 2, hc_dead, n=2)
    done(rb, rn, a)
    rb, rn, rtok = n_c.finish(dg3, n_k.dg_done, 0)
    for k in range(2):
        tb = tmp[k]
        a = dve.do(lambda e, k=k, tb=tb, r=bank(rb, 0, 256): e.scalar_tensor_tensor(
            tb[:, 0:256], ckr[:, k, T:TA], GKVA[:, k:k + 1], r, ALU.mult, ALU.mult),
            ck_t, rtok, tmp_free[k])
        tmp_free[k] = part(tb[:, 0:256], ck[0][:, k, T:TA], ck[1][:, k, T:TA], a, hc_dead)
        ck_tok[k] = ck_tok[k] + tmp_free[k]
    done(rb, rn, a)
    ckr_dead = a
    ga_free[0] = [n_k.sqf, n_c.sqf]
    ga_free[1] = [dg_dead, t_free]
    ga_free[2], ga_free[3] = list(tmp_free), list(tmp_free)
    for j in range(3):
        ga_block(j)

    Q = at("Q", [8, 768], O_X)
    K_ = at("K", [10, 768], O_V + 28 * KB)
    q_t = [None] * 8
    for i3 in range(3):
        tile = W.take()
        for n2 in range(4):
            b = banks(1)
            for i in range(2):
                n = 2 * n2 + i
                for k in range(3):
                    mm3(psum[:, b, 256 * i:256 * i + 256], ch(cq, k, n * P, n * P + P), wt(tile, k, 256),
                        k == 0, k == 2, (tile[2], cq_tok))
            m = pe.mark()
            dst, src = Q[:, 2 * n2:2 * n2 + 2, 256 * i3:256 * i3 + 256], psum[:, b, :].rearrange("p (a c) -> p a c", a=2)
            if n2 % 2:
                t = act.do(lambda e, d=dst, s=src: e.activation(d, s, ACT.Copy), m, cqr_dead, ckr_dead)
            else:
                t = dve.do(lambda e, d=dst, s=src: e.tensor_copy(d, s), m, cqr_dead, ckr_dead)
            done(b, 1, t)
            q_t[2 * n2] = q_t[2 * n2 + 1] = t
        W.release(tile[3], m)
    cq_dead = m
    k_t = [None] * 10
    tile = W.take()
    for n in range(10):
        b = banks(1)
        for k in range(2):
            mm3(psum[:, b, :], ch(ck, k, n * P, n * P + P), wt(tile, k, 512), k == 0, k == 1, (tile[2], ck_tok))
        m = pe.mark()
        kv = K_[:, n, :].rearrange("p (h d) -> p h d", h=8)
        src = psum[:, b, :].rearrange("p (h d) -> p h d", h=8)
        fr = [cq_dead, ga_free[1], n_c.dg_done]
        if n % 2:
            t = act.do(lambda e, d=kv, s=src: e.activation(d[:, :, 0:64], s, ACT.Copy), m, fr)
        else:
            t = dve.do(lambda e, d=kv, s=src: e.tensor_copy(d[:, :, 0:64], s), m, fr)
        done(b, 1, t)
        t2 = pool.do(lambda e, d=kv, n=n: e.tensor_copy(
            d[:, :, 64:96], kpe[:, n, :].unsqueeze(1).to_broadcast([P, 8, 32])), kpe_tok, fr)
        k_t[n] = [t, t2]
    W.release(tile[3], m)

    sA = [at(f"sA{i}", [768], O_X + (24 + 3 * i) * KB) for i in range(2)]
    rot = at("rot", [256], O_V + 58 * KB)
    ss = small[:, 0:80]
    rs8 = at("rs8", [80], O_V + 59 * KB)
    gqs = dve.do(lambda e: e.tensor_scalar(gq[:], gq[:], MLA_SCALE, None, ALU.mult))
    sa_free = [[ga_free[0], t], [ga_free[0], t]]
    rot_free = [None]

    def qk_prep(D, nb, gain, toks, prev):
        rd = []
        for n in range(nb):
            a = act.do(lambda e, n=n: e.activation(sA[n % 2][:], D[:, n, :], ACT.Square), toks[n], sa_free[n % 2])
            t = dve.do(lambda e, n=n: e.tensor_reduce(
                ss[:, 8 * n:8 * n + 8], sA[n % 2][:].rearrange("p (h d) -> p h d", h=8), AX.X, ALU.add), a, prev)
            sa_free[n % 2] = t
        a = act.do(lambda e: e.activation(rs8[:, 0:8 * nb], ss[:, 0:8 * nb], ACT.Sqrt, bias=EPSV, scale=1.0 / 96), t, prev)
        r = dve.do(lambda e: e.reciprocal(rs8[:, 0:8 * nb], rs8[:, 0:8 * nb]), a)
        res = []
        for n in range(nb):
            Dn = D[:, n, :].rearrange("p (h d) -> p h d", h=8)
            t = dve.do(lambda e, Dn=Dn, n=n: e.tensor_tensor(
                Dn, Dn, rs8[:, 8 * n:8 * n + 8].unsqueeze(2).to_broadcast([P, 8, 96]), ALU.mult), r)
            t2 = dve.do(lambda e, Dn=Dn: e.tensor_tensor(
                Dn, Dn, gain[:].unsqueeze(1).to_broadcast([P, 8, 96]), ALU.mult), t, gqs)
            if n >= 8:
                res.append([t2])
                continue
            Dr = Dn[:, :, 64:96].rearrange("p h (a s i) -> p h a s i", a=2, s=2)
            R = rot[:].rearrange("p (h a s i) -> p h a s i", h=8, a=2, s=2)
            tb = rope[:, n, :]
            sn = tb[:, 32:64].rearrange("p (a s i) -> p a s i", a=2, s=2)
            for s in range(2):
                t3 = pool.do(lambda e, s=s, R=R, Dr=Dr, sn=sn: e.tensor_tensor(
                    R[:, :, :, s, :], Dr[:, :, :, 1 - s, :],
                    sn[:, :, s, :].unsqueeze(1).to_broadcast([P, 8, 2, 8]), ALU.mult), t2, rot_free[0])
            t4 = pool.do(lambda e, Dn=Dn, tb=tb: e.tensor_tensor(
                Dn[:, :, 64:96], Dn[:, :, 64:96], tb[:, 0:32].unsqueeze(1).to_broadcast([P, 8, 32]), ALU.mult), t3)
            t5 = pool.do(lambda e, Dn=Dn: e.tensor_tensor(
                Dn[:, :, 64:96], Dn[:, :, 64:96], rot[:].rearrange("p (h d) -> p h d", h=8), ALU.add), t4)
            rot_free[0] = t5
            res.append([t5])
        return res, t2

    rot_free[0] = ga_free[1]
    qn_tok, lastq = qk_prep(Q, 8, gq, q_t, [ga_free[1], sm_free])
    kn_tok, _ = qk_prep(K_, 10, gk, k_t, lastq)
    for j in range(3, 8):
        m = ga_block(j)
    h_dead = m
    V_ = pair("Vv", [10, 768], O_U, O_U + 30 * KB)
    vq = [V_[x][:].rearrange("p n (c a d) -> p n c a d", c=4, a=3) for x in range(2)]
    one_t = [pool.do(lambda e, x=x, n=n: e.memset(f(vq[x][:, n, :, 1, :]), 1.0 - x), h_dead)
             for n in range(10) for x in range(2)]
    tile = W.take()
    vv_tok = [one_t]
    for n in range(10):
        b = banks(1)
        for k in range(2):
            mm3(psum[:, b, :], ch(ck, k, n * P, n * P + P), wt(tile, k, 512), k == 0, k == 1, (tile[2], ck_tok))
        p = part(bank(b).rearrange("p (c a d) -> p c a d", c=4, a=2), vq[0][:, n, :, 0:3:2, :],
                 vq[1][:, n, :, 0:3:2, :], pe.mark(), h_dead)
        done(b, 1, *p)
        vv_tok += p
    ck_dead = pe.mark()
    W.release(tile[3], ck_dead)

    O_HL = O_RING + N_RAW * 4 * KB
    qT = [pair(f"qT{i}", [1024], O_HL + 8 * i * KB, O_HL + (8 * i + 4) * KB) for i in range(2)]
    kT2 = [pair(f"kT2_{i}", [TA], O_V + 10 * i * KB, O_V + (10 * i + 5) * KB) for i in range(2)]
    MX = [at(f"MX{i}", [512], O_HL + (16 + 2 * i) * KB) for i in range(3)]
    MP = [pair("MP0", [512], O_HL + 22 * KB, O_HL + 24 * KB), pair("MP1", [512], O_HL + 26 * KB, O_HL + 28 * KB),
          pair("MP2", [512], O_X + 24 * KB, O_X + 26 * KB)]
    sums = [at(f"sums{i}", [512], O_X + (28 + 2 * i) * KB) for i in range(2)]
    dg4 = at("dg4", [8, P], O_V + 20 * KB)
    old = [h_dead, ck_dead, ga_free, kn_tok]
    for i in range(2):
        for x in range(2):
            kt1 = dve.do(lambda e, i=i, x=x: e.memset(f(kT2[i][x][96:97, :]), 1.0 - x), old)
    qT_free, kT_free = [old, old], [old, old]
    EX_free, EP_free, sum_free = [old] * 3, [old] * 3, [old] * 2
    mxa = small[:, 80:96].rearrange("p (s b) -> p s b", s=2)
    for i in range(8):
        pe.wait(free[i])
    S = psum[:, 0:3, :].rearrange("p b n -> p (b n)")
    S_free, R_free, O_free = [free[0:3]], [free[3], free[4], free[5]], [free[6], free[7]]
    head_tok, max_tok, row_tok = {}, {}, {}
    dg_free = [old]

    def Ocol(c):
        return Q[:, :, 192 * c:192 * c + 128]

    def turn_head(h, who):
        D, nb, dst, fr, toks = ((Q, 8, qT[h % 2], qT_free, qn_tok), (K_, 10, kT2[h % 2], kT_free, kn_tok))[who]
        pe.wait(S_free[0])
        for n in range(nb):
            pe.quiet(lambda e, n=n: e.transpose(
                S[0:96, n * P:n * P + P], D[:, n, 96 * h:96 * h + 96], ident[:]), toks[n])
        q_used[h] = pe.mark()
        p = part(S[0:96, 0:nb * P], dst[0][0:96, 0:nb * P], dst[1][0:96, 0:nb * P], q_used[h], fr[h % 2])
        S_free[0] = p
        head_tok.setdefault(h, []).extend(p)

    def maxima(h, qb):
        pe.wait(S_free[0])
        q = [qT[h % 2][x][0:96, qb * P:qb * P + P] for x in range(2)]
        for c0, c1 in ((0, 512), (512, 1024), (1024, 1280)):
            mm3(S[:, c0:c1], q, [kT2[h % 2][x][0:96, c0:c1] for x in range(2)], True, True, (head_tok[h],))
        t = dve.do(lambda e: e.tensor_reduce(mxa[:, h % 2, qb:qb + 1], S[:, 0:TA], AX.X, ALU.max, negate=True),
                   pe.mark())
        S_free[0] = t
        max_tok[h] = t

    def max_row(h):
        d = dve.do(lambda e: e.tensor_tensor(
            dg4[:], ident[:, None, :].to_broadcast([P, 8, P]),
            mxa[:, h % 2, :].unsqueeze(2).to_broadcast([P, 8, P]), ALU.mult), max_tok[h], dg_free[0])
        pe.wait(S_free[0])
        for i in range(2):
            mm(S[0:97, 512 * i:512 * i + 512], ones[:, 0:97],
               dg4[:, 4 * i:4 * i + 4, :].rearrange("p a b -> p (a b)"), True, True, (d,))
        dg_free[0] = pe.mark()
        p = part(S[96:97, 0:1024], qT[h % 2][0][96:97, :], qT[h % 2][1][96:97, :], dg_free[0], qT_free[h % 2])
        S_free[0] = p
        row_tok[h] = p

    q_used, o_done, later = {}, {}, {}
    units = [(h, hf, kb) for h in range(8) for hf in range(2) for kb in range(10)]
    ex_tok, ep_tok = {}, {}

    def logits(u):
        h, hf, kb = units[u]
        r = 3 + u % 3
        pe.wait(R_free[u % 3])
        mm3(psum[:, r, :], [kT2[h % 2][x][0:97, kb * P:kb * P + P] for x in range(2)],
            [qT[h % 2][x][0:97, 512 * hf:512 * hf + 512] for x in range(2)], True, True,
            (head_tok[h], row_tok[h], kt1))
        m = pe.mark()
        if (hf, kb) == (1, 9):
            qT_free[h % 2] = kT_free[h % 2] = m
        ex_tok[u] = act.do(lambda e: e.activation(MX[u % 3][:], bank(r), ACT.Exp), m, EX_free[u % 3])
        R_free[u % 3] = ex_tok[u]

    def split(u):
        ep_tok[u] = part(MX[u % 3][:], MP[u % 3][0][:], MP[u % 3][1][:], ex_tok[u], EP_free[u % 3],
                         q=pool if u % 3 == 1 else dve)
        EX_free[u % 3] = ep_tok[u]

    def times_v(u):
        h, hf, kb = units[u]
        o = psum[:, 6 + hf, :]
        if kb == 0:
            pe.wait(O_free[hf])
        c0 = 192 * (h // 2) + 64 * (h % 2)
        mm3(o, [V_[x][:, kb, c0:c0 + 128] for x in range(2)], [MP[u % 3][x][:] for x in range(2)],
            kb == 0, kb == 9, (ep_tok[u], vv_tok))
        EP_free[u % 3] = m = pe.mark()
        if kb == 9:
            r0, s0 = (0, 64) if h % 2 == 0 else (64, 0)
            inv = []

            def invert(c):
                inv.append(dve.do(lambda e: e.reciprocal(sums[hf][r0:r0 + 64, 256 * c:256 * c + 256],
                                                         o[s0:s0 + 64, 256 * c:256 * c + 256]), m, sum_free[hf]))

            def scale():
                t = dve.do(lambda e: e.tensor_tensor(
                    Ocol(h // 2)[r0:r0 + 64, 4 * hf:4 * hf + 4, :],
                    o[r0:r0 + 64, :].rearrange("p (b q) -> p b q", b=4),
                    sums[hf][r0:r0 + 64, :].rearrange("p (b q) -> p b q", b=4), ALU.mult),
                    inv, m, q_used[min(7, h + 1)])
                sum_free[hf] = O_free[hf] = t
                o_done[h] = t

            later[u + 1] = lambda: invert(0)
            later[u + 2] = lambda: invert(1)
            later[u + 3] = scale

    beside = {0: lambda h: turn_head(h, 0), 2: lambda h: turn_head(h, 1), 16: max_row}
    for qb, at_ in enumerate((4, 5, 7, 8, 10, 11, 13, 14)):
        beside[at_] = lambda h, qb=qb: maxima(h, qb)
    for i in sorted(beside):
        beside[i](0)
    n_u = len(units)
    logits(0)
    logits(1)
    split(0)
    for u in range(n_u):
        if u + 1 < n_u:
            split(u + 1)
        if u + 2 < n_u:
            logits(u + 2)
        h, i = u // 20 + 1, u % 20
        if h < 8 and i in beside:
            beside[i](h)
        if u in later:
            later.pop(u)()
        times_v(u)
    for u in sorted(later):
        later[u]()
    for i in range(3):
        free[i], free[3 + i] = S_free[0], R_free[i]
    free[6], free[7] = O_free
    all_att = [o_done[7], EP_free]
    W.resume(all_att)

    oT = pair("oT", [4, 1024], O_V + 28 * KB, O_V + 44 * KB)
    oT_tok = []
    for c in range(4):
        oT_tok.append(part(Ocol(c), *(y[:, c, :].rearrange("p (b q) -> p b q", b=8) for y in oT),
                           o_done[7], all_att))
    q_dead = oT_tok
    s_x3 = [sem(f"s_xt{i}") for i in range(4)]
    for i in range(4):
        t = pool.dma(lambda e, i=i: e.dma_start(X[:, 2 * i:2 * i + 2, :], A["x1s"][:, 2 * i:2 * i + 2, :]),
                     s_x3[i], q_dead, all_att, spilled)
        x_tok[2 * i] = x_tok[2 * i + 1] = t
    gal = [at(f"gal{i}", [1024], O_V + 4 * i * KB) for i in range(2)]
    tsl = [at(f"tsl{i}", [1024], O_V + (8 + 4 * i) * KB) for i in range(2)]
    mtm = [at(f"mtm{i}", [1024], O_V + (16 + 4 * i) * KB) for i in range(2)]
    s_gl = [sem(f"s_gl{i}") for i in range(2)]
    s_tl = [sem(f"s_tl{i}") for i in range(2)]
    gl_free, tl_free, mt_free = [all_att] * 2, [all_att] * 2, [all_att] * 2
    gl_tok, tl_tok = {}, {}

    def gates(j):
        i = j % 2
        gl_tok[j] = pool.dma(lambda e: e.dma_start(gal[i][:], A["gas"][j]), s_gl[i], gl_free[i], ga_free)
        tl_tok[j] = pool.dma(lambda e: e.dma_start(tsl[i][:], A["ts"][j]), s_tl[i], tl_free[i], t_free)

    M = pair("M", [8, 1024], O_U, O_U + 32 * KB)
    m_tok = [None] * 8
    gates(0)
    gates(1)
    for j in range(8):
        if j % 2 == 0:
            ao_tile = W.take()
        z = j % 2
        ts = []
        for i, (b, m) in enumerate(proj_T(oT, oT_tok, nk=4, n_w=256, sub=128 * (j % 2), tile=ao_tile)):
            sl = slice(512 * i, 512 * i + 512)
            t = dve.do(lambda e, b=b, sl=sl, z=z: e.tensor_tensor(mtm[z][:, sl], bank(b), gal[z][:, sl], ALU.mult),
                       m, gl_tok[j], mt_free[z])
            done(b, 1, t)
            ts.append(t)
        if j % 2 == 1:
            W.release(ao_tile[3], m)
        gl_free[z] = t
        t = dve.do(lambda e, z=z: e.tensor_tensor(mtm[z][:], mtm[z][:], tsl[z][:], ALU.add), ts, tl_tok[j])
        tl_free[z] = t
        if j < 6:
            gates(j + 2)
        m_tok[j] = part(mtm[z][:], M[0][:, j, :], M[1][:, j, :], t, all_att)
        mt_free[z] = m_tok[j]
    oT_dead = m
    nm = Norm(INV1024, T, sq, oT_dead)
    for n in range(8):
        ts = []
        for i, (b, m) in enumerate(proj_T(M, m_tok)):
            sl = slice(512 * i, 512 * i + 512)
            t = dve.do(lambda e, b=b, sl=sl, n=n: e.scalar_tensor_tensor(
                X[:, n, sl], bank(b), GT1[:, n:n + 1], X[:, n, sl], ALU.mult, ALU.add), m, x_tok[n])
            done(b, 1, t)
            ts.append(t)
        x_tok[n] = ts
        nm.add(X[:, n, :], ts, last=n == 7)
    m_dead = m
    H2 = at("H2", [8, 1024], O_U)
    wr = at("wr", [8, 16], O_CONST + 6144)
    s_wr = sem("s_wr")
    wr_tok = pool.dma(lambda e: e.dma_start(wr[:], A["w_r"]), s_wr)
    tm2 = [at(f"tm2_{i}", [1024], O_V + (16 + 4 * i) * KB) for i in range(2)]
    t2_free = list(mt_free)
    rb, rn, rtok = nm.finish(dg, oT_dead, 0)
    lb = banks(2)
    held.update((lb, lb + 1))
    h2_tok = [None] * 8
    for k in range(8):
        tb = tm2[k % 2]
        a = dve.do(lambda e, k=k, tb=tb, r=two(rb): e.scalar_tensor_tensor(
            tb[:], X[:, k, :], SC2[:, k:k + 1], r, ALU.mult, ALU.mult), rtok, x_tok[k], t2_free[k % 2])
        h2_tok[k] = act.do(lambda e, k=k, tb=tb: e.activation(
            H2[:, k, :], tb[:], ACT.Identity, bias=SH2[:, k:k + 1]), a, m_dead)
        t2_free[k % 2] = h2_tok[k]
        for i in range(2):
            mm(psum[0:16, lb + i, :], wr[:, k, :], H2[:, k, 512 * i:512 * i + 512], k == 0, k == 7, (h2_tok[k], wr_tok))
    done(rb, rn, a)
    lgT = at("lgT", [1024], O_U + 40 * KB)
    t = act.do(lambda e, lb=lb: e.activation(lgT[0:16, :], two(lb)[0:16, :], ACT.Copy), pe.mark(), m_dead)
    held.clear()
    done(lb, 2, t)
    lb = banks(1)
    held.add(lb)
    for n in range(8):
        pe.quiet(lambda e, n=n, lb=lb: e.transpose(
            psum[:, lb, 16 * n:16 * n + 16], lgT[0:16, n * P:n * P + P], ident[0:16, 0:16]), t)
    log_m = pe.mark()
    aff = at("aff", [8, 16], O_U + 44 * KB)
    lg = psum[:, lb, 0:128].rearrange("p (n e) -> p n e", n=8)
    sm8, su8 = small[:, 0:8], small[:, 8:16]
    bc = lambda v: v.unsqueeze(2).to_broadcast([P, 8, 16])
    t = dve.do(lambda e: e.tensor_reduce(sm8, lg, AX.X, ALU.max), log_m, o_done[7])
    t = dve.do(lambda e: e.tensor_tensor(aff[:], lg, bc(sm8), ALU.subtract), t, m_dead)
    done(lb, 1, t)
    held.discard(lb)
    t = act.do(lambda e: e.activation(aff[:], aff[:], ACT.Exp), t)
    t = dve.do(lambda e: e.tensor_reduce(su8, aff[:], AX.X, ALU.add), t)
    t = dve.do(lambda e: e.reciprocal(su8, su8), t)
    aff_t = dve.do(lambda e: e.tensor_tensor(aff[:], aff[:], bc(su8), ALU.mult), t)
    b = banks(2)
    for n in range(8):
        pe.quiet(lambda e, n=n, b=b: e.transpose(
            two(b)[0:16, n * P:n * P + P], aff[:, n, :], ident[:]), aff_t)
    m = pe.mark()
    cur = [at(f"cur{i}", [1024], O_U + (45 + 4 * i) * KB) for i in range(2)]
    vals = at("vals", [128], O_U + 53 * KB)
    idx = at("idx", [128], O_U + 54 * KB, U32)
    idxf = at("idxf", [128], O_U + 55 * KB)
    gcol = at("gcol", [16], O_U + 56 * KB)
    icol = at("icol", [16], O_U + 57 * KB, U32)
    c_t = dve.do(lambda e, b=b: e.tensor_copy(cur[0][0:16, :], two(b)[0:16, :]), m, m_dead)
    done(b, 2, c_t)
    row = [at(f"row{i}", [1024], O_V + (40 + 4 * i) * KB) for i in range(5)]
    s_row = [sem(f"s_row{i}") for i in range(5)]
    row_free = [[oT_dead, nm.m, nm.dg_done, m_dead]] * 5
    nrow = [0]

    def rows(srcs, toks, dram, n):
        i = nrow[0] % 5
        nrow[0] += 1
        b = banks(2)
        for k in range(8):
            pe.quiet(lambda e, k=k, b=b: e.transpose(
                two(b)[:, k * P:k * P + P], srcs[:, k, n * P:n * P + P], ident[:]), toks)
        m = pe.mark()
        t = act.do(lambda e: e.activation(row[i][:], two(b), ACT.Copy), m, row_free[i])
        done(b, 2, t)
        row_free[i] = pool.dma(lambda e: e.dma_start(dram[n * P:n * P + P, :], row[i][:]), s_row[i], t)
        return m

    for n in range(8):
        rows(H2, h2_tok, A["h2s"], n)
    h2_saved = list(row_free)
    for n in range(8):
        x2_m = rows(X, x_tok, out, n)
    rows_saved = list(row_free)

    for r in range(16):
        c0, c1 = cur[r % 2][0:16, :], cur[1 - r % 2][0:16, :]
        v8, i8 = vals[0:16, 8 * r:8 * r + 8], idx[0:16, 8 * r:8 * r + 8]
        t = dve.do(lambda e, v8=v8, c0=c0: e.max(v8, c0), c_t)
        t2 = dve.do(lambda e, v8=v8, c0=c0, i8=i8: e.max_index(i8, v8, c0), t)
        if r < 15:
            c_t = dve.do(lambda e, v8=v8, c0=c0, c1=c1: e.match_replace(c1, v8, c0, -1.0), t2)
    t = dve.do(lambda e: e.tensor_copy(idxf[0:16, :], idx[0:16, :]), t2)
    b = banks(1)
    pe.quiet(lambda e, b=b: e.transpose(psum[:, b, 0:16], vals[0:16, :], ident[0:16, 0:16]), t)
    pe.quiet(lambda e, b=b: e.transpose(psum[:, b, 16:32], idxf[0:16, :], ident[0:16, 0:16]), t)
    m = pe.mark()
    g_t = dve.do(lambda e, b=b: e.tensor_copy(gcol[:], psum[:, b, 0:16]), m)
    i_t = dve.do(lambda e, b=b: e.tensor_copy(icol[:], psum[:, b, 16:32]), m)
    done(b, 1, g_t, i_t)
    grown = [at(f"rawe{i}", [1024], O_V + 4 * i * KB) for i in range(15)]
    s_grown = [sem(f"s_rawe{i}") for i in range(15)]
    gfree = [[m_dead, t2_free, oT_dead, gl_free, tl_free, mt_free] + ([rows_saved] if i >= 10 else []) for i in range(15)]
    gx = [at(f"rawx{i}", [1024], O_X + 4 * i * KB) for i in range(8)]
    s_gx = [sem(f"s_rawx{i}") for i in range(8)]
    W.grow(grown + gx, s_grown + s_gx, gfree + [[x2_m]] * 8)
    W.pool_lo = False

    dg2 = at("dg2", [8, P], O_U + 60 * KB)
    g2b = at("g2b", [1024], O_U + 40 * KB)
    d = dve.do(lambda e: e.tensor_tensor(
        dg2[:], ident[:, None, :].to_broadcast([P, 8, P]), GT2.unsqueeze(2).to_broadcast([P, 8, P]), ALU.mult),
        mod_tok, m_dead)
    b = banks(2)
    for i in range(2):
        mm(psum[:, b + i, :], ones[:], dg2[:, 4 * i:4 * i + 4, :].rearrange("p a b -> p (a b)"), True, True, (d,))
    g2_t = act.do(lambda e, b=b: e.activation(g2b[:], two(b), ACT.Copy), pe.mark(), m_dead)
    done(b, 2, g2_t)

    xg = [at(f"xg{i}", [1024], O_U + 4 * i * KB) for i in range(2)]
    xe = [pair(f"xe{i}", [8, P], O_U + (8 + 8 * i) * KB, O_U + (12 + 8 * i) * KB) for i in range(2)]
    hs = at("hs", [512], O_U + 24 * KB)
    hv = at("hv", [512], O_U + 26 * KB)
    hT = pair("hT", [4, P], O_U + 28 * KB, O_U + 30 * KB)
    ye = [at(f"ye{i}", [1024], O_U + (32 + 4 * i) * KB) for i in range(2)]
    s_xg = [sem(f"s_xg{i}") for i in range(2)]
    s_ye = [sem(f"s_ye{i}") for i in range(2)]
    h2_dead = x2_m
    xg_free, xe_free, ye_free = [h2_dead] * 2, [h2_dead] * 2, [h2_dead] * 2
    xg_tok, xe_tok = {}, {}

    def gather(e_):
        i = e_ % 2
        xg_tok[e_] = pool.dma(lambda e: e.indirect_dma_start(
            out=xg[i][:], out_offset=None, in_=A["h2s"],
            in_offset=bass.IndirectOffsetOnAxis(ap=icol[:, e_:e_ + 1], axis=0)), s_xg[i], xg_free[i], h2_saved, i_t)

    def turn_rows(e_):
        i = e_ % 2
        b = banks(2)
        for k in range(8):
            pe.quiet(lambda e, k=k, b=b: e.transpose(
                two(b)[:, k * P:k * P + P], xg[i][:, k * P:k * P + P], ident[:]), xg_tok[e_])
        m = pe.mark()
        xg_free[i] = m
        x0, x1 = (y[:].rearrange("p a b -> p (a b)") for y in xe[i])
        xe_tok[e_] = part(two(b), x0, x1, m, xe_free[i])
        done(b, 2, *xe_tok[e_])

    gather(0)
    gather(1)
    turn_rows(0)
    hs_free, hv_free, hT_free = h2_dead, h2_dead, h2_dead
    scat = rows_saved
    for e_ in range(16):
        i = e_ % 2
        ba, bb = banks(1), banks(1)
        for c in range(4):
            for bq in (ba, bb):
                tile = W.take()
                for k2 in range(2):
                    k = 2 * c + k2
                    mm3(psum[:, bq, :], (xe[i][0][:, k, :], xe[i][1][:, k, :]), wt(tile, k2, 512),
                        k == 0, k == 7, (tile[2], xe_tok[e_]))
                m = pe.mark()
                W.release(tile[3], m)
                if bq == ba:
                    ma = m
        xe_free[i] = m
        if e_ < 14:
            gather(e_ + 2)
        t = act.do(lambda e, ba=ba: e.activation(hs[:], bank(ba), ACT.Silu), ma, hs_free)
        done(ba, 1, t)
        t = dve.do(lambda e, bb=bb: e.tensor_tensor(hv[:], bank(bb), hs[:], ALU.mult), t, m, hv_free)
        done(bb, 1, t)
        hs_free = t
        if e_ < 15:
            turn_rows(e_ + 1)
        b = banks(1)
        for c in range(4):
            pe.quiet(lambda e, c=c, b=b: e.transpose(psum[:, b, c * P:c * P + P], hv[:, c * P:c * P + P], ident[:]), t)
        m = pe.mark()
        hv_free = m
        y0, y1 = (y[:].rearrange("p a b -> p (a b)") for y in hT)
        hT_t = part(bank(b), y0, y1, m, hT_free)
        done(b, 1, *hT_t)
        b = banks(2)
        for c in range(4):
            tile = W.take()
            for j in range(2):
                mm3(psum[:, b + j, :], (hT[0][:, c, :], hT[1][:, c, :]),
                    (tile[0][:, 512 * j:512 * j + 512], tile[1][:, 512 * j:512 * j + 512]), c == 0, c == 3,
                    (tile[2], hT_t))
            m = pe.mark()
            W.release(tile[3], m)
        hT_free = m
        t = dve.do(lambda e, b=b, i=i, e_=e_: e.scalar_tensor_tensor(
            ye[i][:], two(b), gcol[:, e_:e_ + 1], g2b[:], ALU.mult, ALU.mult), m, g2_t, g_t, ye_free[i])
        done(b, 2, t)
        scat = pool.dma(lambda e, i=i, e_=e_: e.indirect_dma_start(
            out=out, out_offset=bass.IndirectOffsetOnAxis(ap=icol[:, e_:e_ + 1], axis=0),
            in_=ye[i][:], in_offset=None, compute_op=ALU.add), s_ye[i], t, scat)
        ye_free[i] = scat
    finish_program([scat])


def slopes():
    return np.exp2(-8.0 * np.arange(1, 17, dtype=np.float32) / 16).astype(np.float32)


def constants():
    c = {"ident": np.eye(128, dtype=np.float32), "ones": np.ones((128, 128), np.float32)}
    qi, kj = np.arange(128)[:, None], np.arange(256)[None, :]
    dist = (128 + qi - kj).astype(np.float32)
    ok = (dist >= 0) & (dist < 128)
    sl = slopes()
    b = np.stack([np.where(ok, -sl[h] * dist, np.float32(-1e30)) for h in range(16)]).astype(np.float32)
    c["bias"] = np.ascontiguousarray(np.stack([b[:8], b[8:]], 1).transpose(0, 2, 1, 3))
    dist = (np.arange(256)[None, :] - np.arange(128)[:, None]).astype(np.float32)
    ok = (dist >= 0) & (dist < 128)
    b = np.stack([np.where(ok, -sl[h] * dist, np.float32(-1e30)) for h in range(16)]).astype(np.float32)
    c["bias_t"] = np.ascontiguousarray(np.stack([b[:8], b[8:]], 1).transpose(0, 2, 1, 3))
    inv = (1.0 / (np.float32(10000.0) ** (np.arange(8, dtype=np.float32) / np.float32(8)))).astype(np.float32)
    t = np.arange(1024)

    def tab(pos):
        a = pos.astype(np.float32)[:, None] * inv[None]
        return np.concatenate([a, a], -1)

    ang = np.concatenate([tab(t // 64), tab(t % 64)], -1)
    sgn = np.tile(np.concatenate([-np.ones(8), np.ones(8)]), 2).astype(np.float32)
    r = np.concatenate([np.cos(ang), np.sin(ang) * sgn], -1).astype(np.float32)
    c["rope"] = np.ascontiguousarray(r.reshape(8, 128, 64).transpose(1, 0, 2))
    n = np.arange(128)
    a = 2 * np.pi * (np.outer(n, n) % 128) / 128
    s = 1.0 / np.sqrt(1024.0 * 128.0)
    c["dft_c"] = np.concatenate([np.cos(a) * s, np.sin(a) * s], -1).astype(np.float32)
    n = np.arange(1024)
    a = 2 * np.pi * (np.outer(n, n) % 1024) / 1024
    c["dft_t"] = np.concatenate([np.cos(a), -np.sin(a)]).astype(np.float32).reshape(16, 128, 1024)
    return c


def lay_out(x, attn_norm, mlp_norm, final_norm, swa_w_qkv, swa_sinks, swa_w_o, mlp_w_up, mlp_w_down,
            c_2, ctx_2, c_ctx_2, w_mod_2, b_mod_2, norm1_g_2, w_in_2, q_a_norm_g_2, kv_a_norm_g_2,
            w_q_up_2, w_kv_up_2, q_norm_g_2, k_norm_g_2, w_o_attn_2, w_fourier_2, w_out_2, norm2_g_2,
            w_router_2, w_e_gate_2, w_e_up_2, w_e_down_2, **unused):
    c = constants()

    def cols(w, n):
        k, m = w.shape
        return np.ascontiguousarray(
            w.reshape(k // 128, 128, m // n, n).transpose(2, 1, 0, 3).reshape(m // n, 128, k // 128 * n))

    def vec(v):
        return v.reshape(-1, 128).T

    r = dict(c)
    r["xT"] = np.ascontiguousarray(x[0].T.reshape(8, 128, 1024).transpose(1, 0, 2))
    r["ctxT"] = np.ascontiguousarray(ctx_2[0].T.reshape(8, 128, 256).transpose(1, 0, 2))
    v = np.zeros((128, 128), np.float32)
    for a, o in ((attn_norm[0], 0), (mlp_norm[0], 8), (final_norm, 16), (norm1_g_2[0], 24), (norm2_g_2[0], 32),
                 (q_a_norm_g_2[0], 40), (kv_a_norm_g_2[0], 43), (b_mod_2[0], 48)):
        v[:, o:o + a.size // 128] = vec(a)
    pairs = np.arange(16).reshape(2, 8).T.reshape(-1)
    v[:, 96:112] = swa_sinks[0][pairs][None, :]
    v[:, 112:117] = np.array([EPS, 1 / 1024, 1 / 384, 1 / 256, 1 / 96], np.float32)
    r["vec"] = v
    r["gq"] = np.ascontiguousarray(np.broadcast_to(q_norm_g_2[0], (128, 96)))
    r["gk"] = np.ascontiguousarray(np.broadcast_to(k_norm_g_2[0], (128, 96)))
    w = swa_w_qkv[0]
    r["w_k"], r["w_v"] = cols(w[:, 1024:1152], 128), cols(w[:, 1152:1280], 128)
    r["w_q"] = cols(w[:, 0:1024].reshape(1024, 16, 64)[:, pairs].reshape(1024, 1024), 128)
    r["w_so"] = cols(swa_w_o[0].reshape(16, 64, 1024)[pairs].reshape(1024, 1024), 128)
    r["w_up"] = cols(mlp_w_up[0], 128)
    r["w_dn"] = np.ascontiguousarray(
        mlp_w_down[0].reshape(8, 4, 128, 4, 256).transpose(0, 3, 2, 1, 4).reshape(32, 128, 1024))
    r["w_mod"] = np.ascontiguousarray(w_mod_2[0].T.reshape(48, 128, 2, 512).transpose(0, 2, 1, 3).reshape(96, 128, 512))
    r["c_b"] = np.ascontiguousarray(np.broadcast_to(c_2[0], (128, 1024)))
    r["cc_b"] = np.ascontiguousarray(np.broadcast_to(c_ctx_2, (128, 1024)))
    w = w_in_2[0]
    r["w_qa"], r["w_kva"] = cols(w[:, 0:384], 128), cols(w[:, 384:640], 128)
    r["w_kpe"] = cols(w[:, 640:672], 32)
    r["w_f"] = cols(w[:, 672:1184], 128)
    r["w_ga"], r["w_gb"] = cols(w[:, 1184:2208], 128), cols(w[:, 2208:3232], 128)
    r["w_qup"] = cols(w_q_up_2[0], 256)
    w = w_kv_up_2[0].reshape(256, 8, 128)
    r["w_kup"] = cols(w[:, :, :64].reshape(256, 512), 512)
    r["w_vup"] = cols(w[:, :, 64:].reshape(256, 512), 512)
    r["w_ao"], r["w_fo"] = cols(w_o_attn_2[0], 256), cols(w_fourier_2[0], 256)
    r["w_out"] = cols(w_out_2[0], 128)
    r["w_r"] = np.ascontiguousarray(w_router_2[0].reshape(8, 128, 16).transpose(1, 0, 2))
    g = w_e_gate_2[0].reshape(16, 4, 2, 128, 512).transpose(0, 1, 3, 2, 4).reshape(16, 4, 128, 1024)
    u = w_e_up_2[0].reshape(16, 4, 2, 128, 512).transpose(0, 1, 3, 2, 4).reshape(16, 4, 128, 1024)
    d = w_e_down_2[0].reshape(16, 4, 128, 1024)
    r["w_e"] = np.stack([g[:, 0], u[:, 0], g[:, 1], u[:, 1], g[:, 2], u[:, 2], g[:, 3], u[:, 3],
                         d[:, 0], d[:, 1], d[:, 2], d[:, 3]], 1).reshape(192, 128, 1024)
    return r


SCRATCH = {"os": (8, 128, 1024), "x1s": (128, 8, 1024), "ts": (8, 128, 1024), "gas": (8, 128, 1024), "h2s": (1024, 1024)}


def kernel(**inputs):
    import concourse.bacc as _bacc
    from concourse.bass_utils import run_bass_kernel_spmd as _run

    nc = _bacc.Bacc("TRN2", target_bir_lowering=False, num_devices=1)
    arrays, A = {}, {}
    for name, a in lay_out(**{k: np.asarray(v) for k, v in inputs.items()}).items():
        arrays[f"in_{name}"] = a
        A[name] = nc.dram_tensor(f"in_{name}", a.shape, F32, kind="ExternalInput").ap()
    for name, shape in SCRATCH.items():
        A[name] = nc.dram_tensor(name, shape, F32, kind="Internal").ap()
    out = nc.dram_tensor("out_0", (1024, 1024), F32, kind="ExternalOutput").ap()
    build(nc, A, out)
    r = _run(nc, [arrays], core_ids=[0])
    return r.results[0]["out_0"].reshape(1, 1024, 1024)
```
